# Optimizing a Trainium2 kernel written in Bass

```python
import math
import jax, jax.numpy as jnp
from jax import lax
import numpy as np

D_MODEL = 1024
BATCH = 1
SEQ = 256
DEPTH = 2

N_HEADS_MLA = 8
MLA_QK_NOPE = 64
MLA_QK_ROPE = 32
MLA_V = 64
MLA_Q_RANK = 768
MLA_KV_RANK = 256
MLA_QK = MLA_QK_NOPE + MLA_QK_ROPE

N_HEADS_SB = 8
SB_HEAD = 64

N_HEADS_MOBA = 8
MOBA_HEAD = 64
MOBA_BLOCK = 256
MOBA_TOPK = 3
MOBA_Q_CHUNK = 32

Q_BLOCK = 128
ROPE_THETA = 500000.0
PARTIAL_ROPE_DIM = MOBA_HEAD // 4
D_FF = 4 * D_MODEL
N_BRANCH = 3
EPS = 1e-6
NEG_INF = -1e30

W_MLA = N_HEADS_MLA * MLA_V
W_SB = N_HEADS_SB * SB_HEAD
W_MOBA = N_HEADS_MOBA * MOBA_HEAD

IN_SPLITS = (MLA_Q_RANK, MLA_KV_RANK, MLA_QK_ROPE, 3 * W_SB, 3 * W_MOBA, N_BRANCH * D_MODEL)
D_IN = sum(IN_SPLITS)
SPLIT_POINTS = [int(v) for v in np.cumsum(IN_SPLITS)[:-1]]


def rmsnorm(x, g):
    xf = x.astype(jnp.float32)
    y = xf * lax.rsqrt(jnp.mean(xf * xf, axis=-1, keepdims=True) + EPS)
    return y.astype(x.dtype) * g

def modulate(h, shift, scale):
    return h * (1.0 + scale[:, None, :]) + shift[:, None, :]

def rope_tables(positions, rot_dim, dtype):
    inv = ROPE_THETA ** (-jnp.arange(0, rot_dim, 2, dtype=jnp.float32) / rot_dim)
    ang = positions.astype(jnp.float32)[..., None] * inv
    return jnp.cos(ang)[:, None].astype(dtype), jnp.sin(ang)[:, None].astype(dtype)

def apply_rope(x, cos, sin):
    rd = 2 * cos.shape[-1]
    xr, xp = x[..., :rd], x[..., rd:]
    x1, x2 = xr[..., : rd // 2], xr[..., rd // 2:]
    rot = jnp.concatenate([x1 * cos - x2 * sin, x1 * sin + x2 * cos], axis=-1)
    return jnp.concatenate([rot, xp], axis=-1)

def to_heads(t, n_heads):
    b, s, w = t.shape
    return t.reshape(b, s, n_heads, w // n_heads).transpose(0, 2, 1, 3)

def from_heads(t):
    b, h, s, d = t.shape
    return t.transpose(0, 2, 1, 3).reshape(b, s, h * d)

def causal_softmax_attention(q, k, v, scale):
    b, h, s, dq = q.shape
    nq = s // Q_BLOCK
    qb = jnp.moveaxis(q.reshape(b, h, nq, Q_BLOCK, dq), 2, 0)
    kpos = jnp.arange(s)

    def body(args):
        qi, i = args
        sc = jnp.einsum('bhqd,bhkd->bhqk', qi, k).astype(jnp.float32) * scale
        qpos = i * Q_BLOCK + jnp.arange(Q_BLOCK)
        sc = jnp.where(kpos[None, :] <= qpos[:, None], sc, NEG_INF)
        p = jax.nn.softmax(sc, axis=-1).astype(v.dtype)
        return jnp.einsum('bhqk,bhkd->bhqd', p, v)

    o = lax.map(body, (qb, jnp.arange(nq)))
    return jnp.moveaxis(o, 0, 2).reshape(b, h, s, v.shape[-1])

def stick_breaking_attention(q, k, v):
    b, h, s, d = q.shape
    scale = 1.0 / math.sqrt(d)
    nq = s // Q_BLOCK
    qb = jnp.moveaxis(q.reshape(b, h, nq, Q_BLOCK, d), 2, 0)
    kpos = jnp.arange(s)

    def body(args):
        qi, i = args
        z = jnp.einsum('bhqd,bhkd->bhqk', qi, k).astype(jnp.float32) * scale
        qpos = i * Q_BLOCK + jnp.arange(Q_BLOCK)
        past = kpos[None, :] < qpos[:, None]
        log_beta = jax.nn.log_sigmoid(z)
        log_keep = jnp.where(past, jax.nn.log_sigmoid(-z), 0.0)
        later = lax.cumsum(log_keep, axis=3, reverse=True) - log_keep
        a = jnp.where(past, jnp.exp(log_beta + later), 0.0).astype(v.dtype)
        return jnp.einsum('bhqk,bhkd->bhqd', a, v)

    o = lax.map(body, (qb, jnp.arange(nq)))
    return jnp.moveaxis(o, 0, 2).reshape(b, h, s, d)

def moba_attention(q, k, v):
    b, h, s, d = q.shape
    scale = 1.0 / math.sqrt(d)
    nb = -(-s // MOBA_BLOCK)
    pad = nb * MOBA_BLOCK - s
    kb = jnp.pad(k, ((0, 0), (0, 0), (0, pad), (0, 0))).reshape(b, h, nb, MOBA_BLOCK, d)
    vb = jnp.pad(v, ((0, 0), (0, 0), (0, pad), (0, 0))).reshape(b, h, nb, MOBA_BLOCK, d)
    kmean = jnp.mean(kb.astype(jnp.float32), axis=3)

    cur = jnp.arange(s) // MOBA_BLOCK
    gate = jnp.einsum('bhsd,bhnd->bhsn', q.astype(jnp.float32), kmean)
    past_blk = jnp.arange(nb)[None, :] < cur[:, None]
    gate = jnp.where(past_blk, gate, NEG_INF)
    topk = min(MOBA_TOPK, nb)
    _, idx = lax.top_k(gate, topk)
    valid = jnp.arange(topk)[None, :] < cur[:, None]

    nc = s // MOBA_Q_CHUNK
    qc = jnp.moveaxis(q.reshape(b, h, nc, MOBA_Q_CHUNK, d), 2, 0)
    ic = jnp.moveaxis(idx.reshape(b, h, nc, MOBA_Q_CHUNK, topk), 2, 0)
    vc = valid.reshape(nc, MOBA_Q_CHUNK, topk)
    gather = jax.vmap(jax.vmap(lambda blocks, ids: blocks[ids]))

    def body(args):
        qi, ii, vi, ci = args
        kg = gather(kb, ii)
        vg = gather(vb, ii)
        qpos = ci * MOBA_Q_CHUNK + jnp.arange(MOBA_Q_CHUNK)
        s_sel = jnp.einsum('bhqd,bhqnjd->bhqnj', qi, kg).astype(jnp.float32) * scale
        s_sel = jnp.where(vi[:, :, None], s_sel, NEG_INF).reshape(b, h, MOBA_Q_CHUNK, topk * MOBA_BLOCK)
        ob = (ci * MOBA_Q_CHUNK) // MOBA_BLOCK
        k_own = lax.dynamic_index_in_dim(kb, ob, axis=2, keepdims=False)
        v_own = lax.dynamic_index_in_dim(vb, ob, axis=2, keepdims=False)
        s_own = jnp.einsum('bhqd,bhjd->bhqj', qi, k_own).astype(jnp.float32) * scale
        kpos = ob * MOBA_BLOCK + jnp.arange(MOBA_BLOCK)
        s_own = jnp.where(kpos[None, :] <= qpos[:, None], s_own, NEG_INF)
        p = jax.nn.softmax(jnp.concatenate([s_sel, s_own], axis=-1), axis=-1).astype(v.dtype)
        p_sel = p[..., : topk * MOBA_BLOCK].reshape(b, h, MOBA_Q_CHUNK, topk, MOBA_BLOCK)
        p_own = p[..., topk * MOBA_BLOCK:]
        return (jnp.einsum('bhqnj,bhqnjd->bhqd', p_sel, vg)
                + jnp.einsum('bhqj,bhjd->bhqd', p_own, v_own))

    o = lax.map(body, (qc, ic, vc, jnp.arange(nc)))
    return jnp.moveaxis(o, 0, 2).reshape(b, h, s, d)

def first_inputs(seed: int = 0) -> dict:
    key = jax.random.key(seed)
    ks = jax.random.split(key, 24)
    f32 = jnp.float32

    def nrm(k, shape, fan_in):
        return jax.random.normal(k, shape, f32) * (fan_in ** -0.5)

    def gain(k, shape):
        return 1.0 + 0.02 * jax.random.normal(k, shape, f32)

    L = DEPTH
    return {
        "x": jax.random.normal(ks[0], (BATCH, SEQ, D_MODEL), f32),
        "c": jax.random.normal(ks[1], (BATCH, D_MODEL), f32),
        "positions": jnp.broadcast_to(jnp.arange(SEQ, dtype=jnp.int32)[None, :], (BATCH, SEQ)),
        "w_ada": nrm(ks[2], (L, D_MODEL, 6 * D_MODEL), D_MODEL),
        "b_ada": 0.02 * jax.random.normal(ks[3], (L, 6 * D_MODEL), f32),
        "norm1_g": gain(ks[4], (L, D_MODEL)),
        "norm2_g": gain(ks[5], (L, D_MODEL)),
        "w_in": nrm(ks[6], (L, D_MODEL, D_IN), D_MODEL),
        "q_norm_g": gain(ks[7], (L, MLA_Q_RANK)),
        "w_uq": nrm(ks[8], (L, MLA_Q_RANK, N_HEADS_MLA * MLA_QK), MLA_Q_RANK),
        "kv_norm_g": gain(ks[9], (L, MLA_KV_RANK)),
        "w_ukv": nrm(ks[10], (L, MLA_KV_RANK, N_HEADS_MLA * (MLA_QK_NOPE + MLA_V)), MLA_KV_RANK),
        "w_o_mla": nrm(ks[11], (L, W_MLA, D_MODEL), W_MLA),
        "w_o_sb": nrm(ks[12], (L, W_SB, D_MODEL), W_SB),
        "w_o_moba": nrm(ks[13], (L, W_MOBA, D_MODEL), W_MOBA),
        "w_out": nrm(ks[14], (L, D_MODEL, D_MODEL), D_MODEL),
        "w_ff1": nrm(ks[15], (L, D_MODEL, D_FF), D_MODEL),
        "w_ff2": nrm(ks[16], (L, D_FF, D_MODEL), D_FF),
        "final_norm_g": gain(ks[17], (D_MODEL,)),
    }

def first_block(x, c, positions, w_ada, b_ada, norm1_g, norm2_g, w_in, q_norm_g, w_uq,
              kv_norm_g, w_ukv, w_o_mla, w_o_sb, w_o_moba, w_out, w_ff1, w_ff2, final_norm_g):
    b, s, _ = x.shape
    cos_mla, sin_mla = rope_tables(positions, MLA_QK_ROPE, x.dtype)
    cos_mb, sin_mb = rope_tables(positions, PARTIAL_ROPE_DIM, x.dtype)
    c_act = jax.nn.silu(c)
    mla_scale = 1.0 / math.sqrt(MLA_QK)

    for l in range(DEPTH):
        mod = c_act @ w_ada[l] + b_ada[l]
        shift1, scale1, gate1, shift2, scale2, gate2 = jnp.split(mod, 6, axis=-1)

        hdn = modulate(rmsnorm(x, norm1_g[l]), shift1, scale1)
        proj = hdn @ w_in[l]
        q_lat, c_kv, k_pe, sb_qkv, mb_qkv, gates = jnp.split(proj, SPLIT_POINTS, axis=-1)

        q = to_heads(rmsnorm(q_lat, q_norm_g[l]) @ w_uq[l], N_HEADS_MLA)
        q_nope, q_pe = q[..., :MLA_QK_NOPE], q[..., MLA_QK_NOPE:]
        kv = to_heads(rmsnorm(c_kv, kv_norm_g[l]) @ w_ukv[l], N_HEADS_MLA)
        k_nope, v_mla = kv[..., :MLA_QK_NOPE], kv[..., MLA_QK_NOPE:]
        q_pe = apply_rope(q_pe, cos_mla, sin_mla)
        k_pe = apply_rope(k_pe[:, None], cos_mla, sin_mla)
        q_mla = jnp.concatenate([q_nope, q_pe], axis=-1)
        k_mla = jnp.concatenate([k_nope, jnp.broadcast_to(k_pe, k_nope.shape[:3] + (MLA_QK_ROPE,))], axis=-1)
        o_mla = from_heads(causal_softmax_attention(q_mla, k_mla, v_mla, mla_scale))

        q_sb, k_sb, v_sb = [to_heads(t, N_HEADS_SB) for t in jnp.split(sb_qkv, 3, axis=-1)]
        o_sb = from_heads(stick_breaking_attention(q_sb, k_sb, v_sb))

        q_mb, k_mb, v_mb = [to_heads(t, N_HEADS_MOBA) for t in jnp.split(mb_qkv, 3, axis=-1)]
        q_mb = apply_rope(q_mb, cos_mb, sin_mb)
        k_mb = apply_rope(k_mb, cos_mb, sin_mb)
        o_mb = from_heads(moba_attention(q_mb, k_mb, v_mb))

        g_a, g_b, g_c = jnp.split(jax.nn.sigmoid(gates), N_BRANCH, axis=-1)
        merged = (g_a * (o_mla @ w_o_mla[l]) + g_b * (o_sb @ w_o_sb[l])
                  + g_c * (o_mb @ w_o_moba[l]))
        x = x + gate1[:, None, :] * (merged @ w_out[l])

        hdn = modulate(rmsnorm(x, norm2_g[l]), shift2, scale2)
        ff = jnp.square(jax.nn.relu(hdn @ w_ff1[l])) @ w_ff2[l]
        x = x + gate2[:, None, :] * ff

    return rmsnorm(x, final_norm_g)


N_A_LAYERS = DEPTH // 2
N_B_LAYERS = DEPTH - N_A_LAYERS
N_DENSE = (DEPTH + 1) // 2
N_MOE = DEPTH // 2

ROPE_THETA_2 = 10000.0
LN_EPS = 1e-5
DN_ALPHA = (2.0 * DEPTH) ** 0.25
DN_BETA = (8.0 * DEPTH) ** -0.25

RET_HEADS = 4
RET_DK = D_MODEL // RET_HEADS
RET_DV = 2 * RET_DK
RET_CHUNK = 128

NSA_HEADS = 16
NSA_GROUPS = 4
NSA_HD = D_MODEL // NSA_HEADS
CMP_LEN = 32
CMP_STRIDE = 16
CMP_HID = 4 * NSA_HD
SLC_LEN = 64
SLC_TOPK = 8
WIN = 512
NSA_QBLK = 32
FORCE_SCORE = 1e9

D_FF_2 = 2816
N_EXPERTS = 8
TOP_K = 2
D_FF_E = 3584


def rotary(x, pos):
    d = x.shape[-1]
    inv = 1.0 / (ROPE_THETA_2 ** (jnp.arange(0, d, 2, dtype=jnp.float32) / d))
    ang = pos.astype(jnp.float32)[:, None] * inv[None, :]
    cos, sin = jnp.cos(ang), jnp.sin(ang)
    xf = x.astype(jnp.float32)
    x1, x2 = xf[..., : d // 2], xf[..., d // 2:]
    return jnp.concatenate([x1 * cos - x2 * sin, x1 * sin + x2 * cos], axis=-1).astype(x.dtype)

def layer_norm(x, g, b):
    xf = x.astype(jnp.float32)
    mu = jnp.mean(xf, -1, keepdims=True)
    var = jnp.mean(jnp.square(xf - mu), -1, keepdims=True)
    return ((xf - mu) * lax.rsqrt(var + LN_EPS) * g + b).astype(x.dtype)

def masked_softmax(s, valid):
    s = jnp.where(valid, s.astype(jnp.float32), -jnp.inf)
    m = jnp.max(s, -1, keepdims=True)
    m = jnp.where(jnp.isfinite(m), m, 0.0)
    e = jnp.where(valid, jnp.exp(s - m), 0.0)
    return e / jnp.maximum(jnp.sum(e, -1, keepdims=True), 1e-30)

def swiglu(x, w_in, w_out):
    a, b = jnp.split(x @ w_in, 2, axis=-1)
    return (jax.nn.silu(a) * b) @ w_out

def retention(x, w_in, gn_g, w_out):
    B, S, _ = x.shape
    H, dk, dv, C = RET_HEADS, RET_DK, RET_DV, RET_CHUNK
    N = S // C
    proj = x @ w_in
    q, k, v, g = jnp.split(proj, [H * dk, 2 * H * dk, 2 * H * dk + H * dv], axis=-1)
    pos = jnp.arange(S)
    q = rotary(q.reshape(B, S, H, dk).transpose(0, 2, 1, 3), pos)
    k = rotary(k.reshape(B, S, H, dk).transpose(0, 2, 1, 3), pos) * dk ** -0.5
    v = v.reshape(B, S, H, dv).transpose(0, 2, 1, 3)
    log_gamma = jnp.log1p(-(2.0 ** (-5.0 - jnp.arange(H, dtype=jnp.float32))))
    i = jnp.arange(C, dtype=jnp.float32)
    rel = i[:, None] - i[None, :]
    intra_decay = jnp.where(rel >= 0, jnp.exp(log_gamma[:, None, None] * jnp.maximum(rel, 0.0)), 0.0)
    q_decay = jnp.exp(log_gamma[:, None] * (i + 1.0))[None, :, :, None]
    k_decay = jnp.exp(log_gamma[:, None] * (C - 1.0 - i))[None, :, :, None]
    chunk_decay = jnp.exp(log_gamma * C)[None, :, None, None]

    def to_chunks(t):
        return t.reshape(B, H, N, C, t.shape[-1]).transpose(2, 0, 1, 3, 4)

    def step(state, inp):
        qi, ki, vi = inp
        scores = jnp.einsum('bhqd,bhkd->bhqk', qi, ki) * intra_decay
        inner = jnp.einsum('bhqk,bhkv->bhqv', scores, vi)
        cross = jnp.einsum('bhqd,bhdv->bhqv', qi, state) * q_decay
        new_state = state * chunk_decay + jnp.einsum('bhkd,bhkv->bhdv', ki * k_decay, vi)
        return new_state, inner + cross

    state0 = jnp.zeros((B, H, dk, dv), jnp.float32)
    _, out = lax.scan(step, state0, (to_chunks(q), to_chunks(k), to_chunks(v)))
    out = out.transpose(1, 2, 0, 3, 4).reshape(B, H, S, dv).astype(jnp.float32)
    mu = jnp.mean(out, -1, keepdims=True)
    var = jnp.mean(jnp.square(out - mu), -1, keepdims=True)
    normed = (out - mu) * lax.rsqrt(var + LN_EPS) * gn_g.reshape(H, 1, dv)
    normed = normed.transpose(0, 2, 1, 3).reshape(B, S, H * dv)
    y = jax.nn.silu(g.astype(jnp.float32)) * normed
    return (y @ w_out).astype(x.dtype)

def nsa_shared_kv(h, w_kv, ck_pe, ck_w1, ck_w2, cv_pe, cv_w1, cv_w2):
    B, S, _ = h.shape
    G, dh = NSA_GROUPS, NSA_HD
    kv = (h @ w_kv).reshape(B, S, 6, G, dh).transpose(2, 0, 3, 1, 4)
    pos = jnp.arange(S)
    k_cmp, v_cmp = rotary(kv[0], pos), kv[1]
    k_slc, v_slc = rotary(kv[2], pos), kv[3]
    k_win, v_win = rotary(kv[4], pos), kv[5]
    n_cmp = (S - CMP_LEN) // CMP_STRIDE + 1
    idx = jnp.arange(n_cmp)[:, None] * CMP_STRIDE + jnp.arange(CMP_LEN)[None, :]

    def compress(t, pe, w1, w2):
        blocks = t[:, :, idx, :] + pe
        flat = blocks.reshape(B, G, n_cmp, CMP_LEN * dh)
        return jax.nn.gelu(flat @ w1) @ w2

    k_c = compress(k_cmp, ck_pe, ck_w1, ck_w2)
    v_c = compress(v_cmp, cv_pe, cv_w1, cv_w2)
    n_slc = S // SLC_LEN
    k_s = k_slc.reshape(B, G, n_slc, SLC_LEN, dh)
    v_s = v_slc.reshape(B, G, n_slc, SLC_LEN, dh)
    pad = ((0, 0), (0, 0), (WIN, 0), (0, 0))
    k_w = jnp.pad(k_win, pad)
    v_w = jnp.pad(v_win, pad)
    return (k_c, v_c, k_s, v_s, k_w, v_w)

def nsa_attention(x, w_q, w_out, k_c, v_c, k_s, v_s, k_w, v_w):
    B, S, _ = x.shape
    H, G, dh = NSA_HEADS, NSA_GROUPS, NSA_HD
    R = H // G
    Q = NSA_QBLK
    proj = x @ w_q
    q = proj[..., : H * dh].reshape(B, S, G, R, dh).transpose(0, 2, 3, 1, 4)
    q = rotary(q, jnp.arange(S)) * dh ** -0.5
    gates = jax.nn.sigmoid(proj[..., H * dh:].astype(jnp.float32))
    gates = gates.reshape(B, S, G, R, 3).transpose(0, 2, 3, 1, 4)
    n_cmp = k_c.shape[2]
    n_slc = k_s.shape[2]
    n_top = min(SLC_TOPK, n_slc)
    cmp_start = jnp.arange(n_cmp) * CMP_STRIDE
    cmp_end = cmp_start + CMP_LEN - 1
    slc_start = jnp.arange(n_slc) * SLC_LEN
    overlap = jnp.clip(jnp.minimum(cmp_start[:, None] + CMP_LEN, slc_start[None, :] + SLC_LEN)
                       - jnp.maximum(cmp_start[:, None], slc_start[None, :]), 0).astype(jnp.float32) / CMP_STRIDE
    j_idx = jnp.arange(n_slc)
    bi = jnp.arange(B)[:, None, None, None]
    gi = jnp.arange(G)[None, :, None, None]

    def block(i):
        s0 = i * Q
        t = s0 + jnp.arange(Q)
        qb = lax.dynamic_slice_in_dim(q, s0, Q, axis=3)
        gb = lax.dynamic_slice_in_dim(gates, s0, Q, axis=3)
        sc = jnp.einsum('bgrqd,bgnd->bgrqn', qb, k_c)
        p_cmp = masked_softmax(sc, cmp_end[None, :] <= t[:, None])
        o_cmp = jnp.einsum('bgrqn,bgnd->bgrqd', p_cmp, v_c)
        imp = jnp.einsum('bgrqn,nj->bgqj', p_cmp, overlap)
        cur = t // SLC_LEN
        forced = (j_idx[None, :] == 0) | (j_idx[None, :] == cur[:, None]) | (j_idx[None, :] == cur[:, None] - 1)
        imp = jnp.where(forced, FORCE_SCORE, imp)
        imp = jnp.where(j_idx[None, :] <= cur[:, None], imp, -jnp.inf)
        top_val, top_idx = lax.top_k(imp, n_top)
        sel_ok = jnp.isfinite(top_val)
        ksel = k_s[bi, gi, top_idx]
        vsel = v_s[bi, gi, top_idx]
        tok = top_idx[..., None] * SLC_LEN + jnp.arange(SLC_LEN)
        valid_s = sel_ok[..., None] & (tok <= t[None, None, :, None, None])
        ss = jnp.einsum('bgrqd,bgqkld->bgrqkl', qb, ksel).reshape(B, G, R, Q, n_top * SLC_LEN)
        p_s = masked_softmax(ss, valid_s.reshape(B, G, 1, Q, n_top * SLC_LEN))
        o_slc = jnp.einsum('bgrqkl,bgqkld->bgrqd', p_s.reshape(B, G, R, Q, n_top, SLC_LEN), vsel)
        kw = lax.dynamic_slice_in_dim(k_w, s0, Q + WIN, axis=2)
        vw = lax.dynamic_slice_in_dim(v_w, s0, Q + WIN, axis=2)
        kpos = s0 - WIN + jnp.arange(Q + WIN)
        valid_w = (kpos[None, :] <= t[:, None]) & (kpos[None, :] > t[:, None] - WIN) & (kpos[None, :] >= 0)
        sw = jnp.einsum('bgrqd,bgkd->bgrqk', qb, kw)
        o_win = jnp.einsum('bgrqk,bgkd->bgrqd', masked_softmax(sw, valid_w), vw)
        return gb[..., 0:1] * o_cmp + gb[..., 1:2] * o_slc + gb[..., 2:3] * o_win

    out = lax.map(block, jnp.arange(S // Q))
    out = out.transpose(1, 0, 4, 2, 3, 5).reshape(B, S, H * dh)
    return (out @ w_out).astype(x.dtype)

def moe_swiglu(x, w_router, w_in, w_out):
    B, S, D = x.shape
    xf = x.reshape(B * S, D)
    logits = (xf @ w_router).astype(jnp.float32)
    top_v, top_i = lax.top_k(logits, TOP_K)
    w = jax.nn.softmax(top_v, axis=-1)
    gate = jnp.sum(jax.nn.one_hot(top_i, N_EXPERTS, dtype=jnp.float32) * w[..., None], axis=1)
    out = jnp.zeros((B * S, D), jnp.float32)
    for e in range(N_EXPERTS):
        out = out + gate[:, e:e + 1] * swiglu(xf, w_in[e], w_out[e])
    return out.reshape(B, S, D).astype(x.dtype)

def second_inputs(seed: int = 0) -> dict:
    key = jax.random.key(seed)
    ks = jax.random.split(key, 20)

    def nrm(k, shape, scale):
        return jax.random.normal(k, shape, jnp.float32) * scale

    ret_qk = RET_HEADS * RET_DK
    ret_v = RET_HEADS * RET_DV
    nsa_q = NSA_HEADS * NSA_HD
    return {
        'x': nrm(ks[0], (BATCH, SEQ, D_MODEL), 1.0),
        'ret_w_in': nrm(ks[1], (N_A_LAYERS, D_MODEL, 2 * ret_qk + 2 * ret_v), D_MODEL ** -0.5),
        'ret_gn_g': 1.0 + nrm(ks[2], (N_A_LAYERS, ret_v), 0.02),
        'ret_w_out': nrm(ks[3], (N_A_LAYERS, ret_v, D_MODEL), DN_BETA * ret_v ** -0.5),
        'nsa_w_kv': nrm(ks[4], (D_MODEL, 6 * NSA_GROUPS * NSA_HD), D_MODEL ** -0.5),
        'cmp_k_pe': nrm(ks[5], (CMP_LEN, NSA_HD), 0.1),
        'cmp_k_w1': nrm(ks[6], (CMP_LEN * NSA_HD, CMP_HID), (CMP_LEN * NSA_HD) ** -0.5),
        'cmp_k_w2': nrm(ks[7], (CMP_HID, NSA_HD), CMP_HID ** -0.5),
        'cmp_v_pe': nrm(ks[8], (CMP_LEN, NSA_HD), 0.1),
        'cmp_v_w1': nrm(ks[9], (CMP_LEN * NSA_HD, CMP_HID), (CMP_LEN * NSA_HD) ** -0.5),
        'cmp_v_w2': nrm(ks[10], (CMP_HID, NSA_HD), CMP_HID ** -0.5),
        'nsa_w_q': nrm(ks[11], (N_B_LAYERS, D_MODEL, nsa_q + 3 * NSA_HEADS), D_MODEL ** -0.5),
        'nsa_w_out': nrm(ks[12], (N_B_LAYERS, nsa_q, D_MODEL), DN_BETA * nsa_q ** -0.5),
        'ffn_w_in': nrm(ks[13], (N_DENSE, D_MODEL, 2 * D_FF_2), D_MODEL ** -0.5),
        'ffn_w_out': nrm(ks[14], (N_DENSE, D_FF_2, D_MODEL), DN_BETA * D_FF_2 ** -0.5),
        'moe_router': nrm(ks[15], (N_MOE, D_MODEL, N_EXPERTS), D_MODEL ** -0.5),
        'moe_w_in': nrm(ks[16], (N_MOE, N_EXPERTS, D_MODEL, 2 * D_FF_E), D_MODEL ** -0.5),
        'moe_w_out': nrm(ks[17], (N_MOE, N_EXPERTS, D_FF_E, D_MODEL), DN_BETA * D_FF_E ** -0.5),
        'ln_g': 1.0 + nrm(ks[18], (DEPTH, 2, D_MODEL), 0.02),
        'ln_b': nrm(ks[19], (DEPTH, 2, D_MODEL), 0.02),
    }

def second_block(x, ret_w_in, ret_gn_g, ret_w_out, nsa_w_kv, cmp_k_pe, cmp_k_w1, cmp_k_w2,
              cmp_v_pe, cmp_v_w1, cmp_v_w2, nsa_w_q, nsa_w_out, ffn_w_in, ffn_w_out,
              moe_router, moe_w_in, moe_w_out, ln_g, ln_b):
    shared = None
    for l in range(DEPTH):
        if l < N_A_LAYERS:
            mix = retention(x, ret_w_in[l], ret_gn_g[l], ret_w_out[l])
        else:
            if l == N_A_LAYERS:
                shared = nsa_shared_kv(x, nsa_w_kv, cmp_k_pe, cmp_k_w1, cmp_k_w2,
                                       cmp_v_pe, cmp_v_w1, cmp_v_w2)
            jb = l - N_A_LAYERS
            mix = nsa_attention(x, nsa_w_q[jb], nsa_w_out[jb], *shared)
        x = layer_norm(DN_ALPHA * x + mix, ln_g[l, 0], ln_b[l, 0])
        if l % 2 == 0:
            f = swiglu(x, ffn_w_in[l // 2], ffn_w_out[l // 2])
        else:
            f = moe_swiglu(x, moe_router[l // 2], moe_w_in[l // 2], moe_w_out[l // 2])
        x = layer_norm(DN_ALPHA * x + f, ln_g[l, 1], ln_b[l, 1])
    return x


def setup_inputs(seed=0):
    out = dict(first_inputs(seed))
    for name, value in second_inputs(seed + 1).items():
        if name != "x":
            out[name + "_2"] = value
    return out


def reference(
    x, c, positions, w_ada, b_ada, norm1_g, norm2_g, w_in, q_norm_g, w_uq, kv_norm_g, w_ukv,
    w_o_mla, w_o_sb, w_o_moba, w_out, w_ff1, w_ff2, final_norm_g, ret_w_in_2, ret_gn_g_2,
    ret_w_out_2, nsa_w_kv_2, cmp_k_pe_2, cmp_k_w1_2, cmp_k_w2_2, cmp_v_pe_2, cmp_v_w1_2,
    cmp_v_w2_2, nsa_w_q_2, nsa_w_out_2, ffn_w_in_2, ffn_w_out_2, moe_router_2, moe_w_in_2,
    moe_w_out_2, ln_g_2, ln_b_2,
):
    x = first_block(
        x, c, positions, w_ada, b_ada, norm1_g, norm2_g, w_in, q_norm_g, w_uq, kv_norm_g, w_ukv,
        w_o_mla, w_o_sb, w_o_moba, w_out, w_ff1, w_ff2, final_norm_g,
    )
    return second_block(
        x, ret_w_in_2, ret_gn_g_2, ret_w_out_2, nsa_w_kv_2, cmp_k_pe_2, cmp_k_w1_2, cmp_k_w2_2,
        cmp_v_pe_2, cmp_v_w1_2, cmp_v_w2_2, nsa_w_q_2, nsa_w_out_2, ffn_w_in_2, ffn_w_out_2,
        moe_router_2, moe_w_in_2, moe_w_out_2, ln_g_2, ln_b_2,
    )


_drawn_inputs = setup_inputs


def setup_inputs(seed=0):
    import zlib

    import numpy as np

    out = dict(_drawn_inputs(seed))
    spreads = {}
    factors = {'norm1_g': 3.93,
     'q_norm_g': 8.0,
     'kv_norm_g': 8.0,
     'ret_gn_g_2': 17.796,
     'cmp_k_pe_2': 8.0,
     'cmp_k_w1_2': 2.858,
     'cmp_v_pe_2': 3.748}
    for name, (base, spread) in spreads.items():
        noise = np.random.default_rng([zlib.crc32(name.encode()), seed]).standard_normal(out[name].shape)
        drawn = base * np.exp(spread * noise) if base else spread * noise
        out[name] = __import__('jax').numpy.asarray(drawn.astype(out[name].dtype))
    for name, factor in factors.items():
        out[name] = (out[name] * factor).astype(out[name].dtype)
    return out
```

```python
from contextlib import ExitStack

import numpy as np
import concourse.bass as bass
from concourse import mybir

F32 = mybir.dt.float32
F32R = mybir.dt.float32r
BF16 = mybir.dt.bfloat16
I32 = mybir.dt.int32
ALU = mybir.AluOpType
ACT = mybir.ActivationFunctionType
AX = mybir.AxisListType.X

P = 128
S = 256
NT = S // P
D = 1024
DEPTH = 2
RING = 4
LEAD = 3
UROWS = 2
UCOLS = 512
USIZE = UROWS * UCOLS
KB = D // P
HD = 64
NH = 8

Q_RANK, KV_RANK, ROPE = 768, 256, 32
MLA_QK = 96
IN_SB = Q_RANK + KV_RANK + ROPE
IN_MB = IN_SB + 3 * 512
IN_GATES = IN_MB + 3 * 512
D_FF = 4096
EPS, LN_EPS = 1e-6, 1e-5
NEG = -1e30
ALPHA = (2.0 * DEPTH) ** 0.25

RET_H, RET_DK, RET_DV = 4, 256, 512
NSA_H, NSA_G = 16, 4
CMP_LEN, CMP_STRIDE, N_CMP, CMP_HID = 32, 16, 15, 256
D_FF2, N_EXP, D_FFE = 2816, 8, 3584
RELU2, SWIGLU, EXPERT = (512, 4, 1, 2), (256, 4, 2, 2), (512, 8, 1, 1)
CAP = 128

HEAD_GROUPS = [(0, 0, NH), (1, 0, NH // 2), (1, NH // 2, NH // 2)]

TWO_PI = 2.0 * np.pi

CONST_WIDTHS = [("ident", P), ("later", P), ("ones", P), ("earlier", P), ("causal", 2 * P), ("iota", P),
                ("cmp_mask", 2 * N_CMP), ("cmp_valid", 2 * N_CMP), ("ret_cos", 2 * P), ("ret_sin", 2 * P),
                ("nsa_cos", 64), ("nsa_sin", 64), ("inv_mla", 16), ("inv_mb", 8), ("lower_index", 64), ("eps", 1), ("not_earlier", P)]
CONST_AT, _n = {}, 0
for _name, _w in CONST_WIDTHS:
    CONST_AT[_name] = (_n, _n + _w)
    _n += _w
NCONST = _n


def shape_constants():
    f = np.float32
    p, q = np.arange(P)[:, None], np.arange(P)[None, :]
    tok = np.arange(S, dtype=f)

    def table(freqs, fn):
        ang = tok[:, None] * freqs[None, :]
        return fn(ang).astype(f).reshape(NT, P, -1).transpose(1, 0, 2).reshape(P, -1)

    ret_inv = (1.0 / (f(10000.0) ** (np.arange(0, RET_DK, 2, dtype=f) / f(RET_DK)))).astype(f)
    nsa_inv = (1.0 / (f(10000.0) ** (np.arange(0, HD, 2, dtype=f) / f(HD)))).astype(f)
    end = np.arange(N_CMP) * CMP_STRIDE + CMP_LEN - 1
    seen = (end[None, :] <= np.arange(S)[:, None]).reshape(NT, P, N_CMP).transpose(1, 0, 2).reshape(P, -1)
    e = np.arange(N_EXP)
    parts = {
        "ident": p == q, "later": p > q, "ones": np.ones((P, P)), "earlier": p < q,
        "causal": np.concatenate([np.zeros((P, P)), np.where(q <= p, 0.0, NEG)], 1),
        "iota": np.broadcast_to(q, (P, P)),
        "cmp_mask": np.where(seen, 0.0, NEG), "cmp_valid": seen,
        "ret_cos": table(ret_inv, np.cos), "ret_sin": table(ret_inv, np.sin),
        "nsa_cos": table(nsa_inv, np.cos), "nsa_sin": table(nsa_inv, np.sin),
        "inv_mla": np.broadcast_to(f(500000.0) ** (-np.arange(0, 32, 2, dtype=f) / f(32)), (P, 16)),
        "inv_mb": np.broadcast_to(f(500000.0) ** (-np.arange(0, 16, 2, dtype=f) / f(16)), (P, 8)),
        "not_earlier": np.where(p < q, 0.0, NEG),
        "eps": np.full((P, 1), EPS),
        "lower_index": np.broadcast_to((e[None, :] < e[:, None]).reshape(1, -1), (P, 64)),
    }
    const = np.concatenate([np.asarray(parts[n], f) for n, _ in CONST_WIDTHS], axis=1)
    lg = np.log1p(-(2.0 ** (-5.0 - np.arange(RET_H))))
    rel = np.stack([q - p, q - p + P], 1)[:, None]
    decay = np.where(rel >= 0, np.exp(lg[None, :, None, None] * np.maximum(rel, 0)), 0.0)
    return const, np.ascontiguousarray(decay.astype(f).reshape(P, -1))


class Counts:

    def __init__(self):
        self.n, self.loops = {}, []

    def at(self, name, more=0):
        v = self.n.get(name, 0) + more
        for reg, stride in self.loops:
            if stride.get(name):
                v = reg * stride[name] + v
        return v

    def add(self, name, k=1):
        self.n[name] = self.n.get(name, 0) + k

    def slot(self, ahead=0):
        k = self.n.get("unit", 0) + ahead
        v = k // RING
        for reg, stride in self.loops:
            assert stride.get("unit", 0) % RING == 0
            if stride.get("unit"):
                v = reg * (stride["unit"] // RING) + v
        return k % RING, v

    def parity(self, name):
        assert all(s.get(name, 0) % 2 == 0 for _, s in self.loops)
        return self.n.get(name, 0) % 2


class Silent:

    def _nothing(self, *a, **k):
        return self

    wait_ge = sem_inc = then_inc = drain = matmul = transpose = activation = dma_start = _nothing
    tensor_tensor = tensor_scalar = scalar_tensor_tensor = tensor_copy = tensor_reduce = _nothing
    tensor_tensor_reduce = reciprocal = memset = bn_stats = bn_aggr = _nothing


SILENT = Silent()


def loop(e, c, n, body):
    before, loops = dict(c.n), c.loops
    c.loops = []
    body(SILENT, 0)
    stride = {k: v - before.get(k, 0) for k, v in c.n.items() if v != before.get(k, 0)}
    c.n, c.loops = dict(before), loops
    if e is not SILENT:
        with e.Fori(0, n) as i:
            c.loops.append((i, stride))
            body(e, i)
            c.loops.pop()
    c.n = dict(before)
    if isinstance(n, int):
        for k, v in stride.items():
            c.add(k, n * v)


def program(nc, a, consts, decays, out):
    ctx = ExitStack()
    with ctx:
        def sb(name, shape, dt=F32):
            return ctx.enter_context(nc.sbuf_tensor(name, shape, dt))

        def sem(name):
            return ctx.enter_context(nc.semaphore(name))

        raw = sb("raw", [P, RING, USIZE])
        whi = sb("whi", [P, RING, USIZE], F32R)
        wlo = sb("wlo", [P, RING, USIZE], F32R)
        const = sb("const", [P, NCONST])
        x = sb("x", [P, NT, D])
        work = sb("work", [P, NT, D])
        xh = sb("xh", [P, KB, S], F32R)
        xl = sb("xl", [P, KB, S], F32R)
        yh = sb("yh", [P, KB, S], F32R)
        yl = sb("yl", [P, KB, S], F32R)
        chi = sb("chi", [P, KB, P], F32R)
        clo = sb("clo", [P, KB, P], F32R)
        mod_a = sb("mod_a", [P, 3 * D])
        mod_b = sb("mod_b", [P, 3 * D])
        gain_a = sb("gain_a", [P, D])
        gain_b = sb("gain_b", [P, D])
        att = sb("att", [P, 6144])
        rope_tab = sb("rope_tab", [P, NT, 2 * (16 + 8)])
        st = sb("st", [P, 160])
        nmax = sb("nmax", [P, 16])
        rsum = sb("rsum", [P, 16])
        zero = sb("zero", [1, UCOLS], BF16)
        posi = sb("posi", [P, NT], I32)
        rounds = sb("rounds", [1, 1], I32)
        ps = ctx.enter_context(nc.psum_tensor("ps", [P, 8, 512], F32))
        with ExitStack() as attentions:
            proj = attentions.enter_context(nc.sbuf_tensor("proj", [P, NT, 2560], F32))
            qT = attentions.enter_context(nc.sbuf_tensor("qT", [P, NH, S], F32))
            kT = attentions.enter_context(nc.sbuf_tensor("kT", [P, NH, S], F32))
        gathered = [[sb(f"gathered_{part}{b}", [P, KB, P], F32R) for part in ("hi", "lo")] for b in range(2)]
        hidden_e = [sb(f"hidden_{part}", [P, 4, P], F32R) for part in ("hi", "lo")]
        onehot = [sb(f"onehot{b}", [P, NT, P], F32R) for b in range(2)]
        onehotT = [sb(f"onehotT{b}", [P, S], F32R) for b in range(2)]
        router_h, router_l = (sb(f"router_{part}", [P, KB, N_EXP], F32R)[:, :, :] for part in ("hi", "lo"))

        def k_(name):
            return const[:, CONST_AT[name][0]:CONST_AT[name][1]]

        ident = k_("ident")

        raw_ready = [sem(f"raw_ready{i}") for i in range(RING)]
        split_hi = sem("split_hi")
        split_lo = sem("split_lo")
        unit_used = sem("unit_used")
        evac_act = sem("evac_act")
        evac_dve = sem("evac_dve")
        t_ready = sem("t_ready")
        t_hi = sem("t_hi")
        t_lo = sem("t_lo")
        job_ready = sem("job_ready")
        job_act = sem("job_act")
        job_dve = sem("job_dve")
        src_ready = sem("src_ready")
        vec_ready = sem("vec_ready")
        act_ready = sem("act_ready")
        score_ready = sem("score_ready")
        prob_ready = sem("prob_ready")
        pv_ready = sem("pv_ready")
        comb_ready = sem("comb_ready")
        comb_free = sem("comb_free")
        gain_a_ready, gain_b_ready = sem("gain_a_ready"), sem("gain_b_ready")
        gain_a_used, gain_b_used = sem("gain_a_used"), sem("gain_b_used")
        bias_ready = [sem(f"bias_ready{i}") for i in range(3)]
        bias_used = [sem(f"bias_used{i}") for i in range(3)]
        out_hi, out_lo = sem("out_hi"), sem("out_lo")
        pool_tick, pe_tick, dve_tick = sem("pool_tick"), sem("pe_tick"), sem("dve_tick")
        const_ready, x_ready, c_ready = sem("const_ready"), sem("x_ready"), sem("c_ready")
        positions_ready = sem("positions_ready")
        zero_ready = sem("zero_ready")
        extra_ready = sem("extra_ready")
        stored = sem("stored")

        prob = [att[:, 0:1024].rearrange("p (h k) -> p h k", h=NH),
                att[:, 1024:3072].rearrange("p (h k) -> p h k", h=NH)]
        heads_out = att[:, 0:1024].rearrange("p (t n) -> p t n", t=NT)
        probT = att[:, 3072:6144].rearrange("p (h b k) -> p h b k", h=NH, b=3)
        q_up = att[:, 0:1536].rearrange("p (t n) -> p t n", t=NT)
        k_cat = att[:, 3072:4608].rearrange("p (t n) -> p t n", t=NT)
        act_tmp = att[:, 0:1024].rearrange("p (t n) -> p t n", t=NT)
        hidden = att[:, 1024:2048].rearrange("p (t n) -> p t n", t=NT)
        eh = chi[:, :, :].rearrange("p k n -> p (k n)")
        el = clo[:, :, :].rearrange("p k n -> p (k n)")
        xth = yh[:, :, :].rearrange("p k s -> p (k s)").rearrange("p (t n) -> p t n", t=NT)
        xtl = yl[:, :, :].rearrange("p k s -> p (k s)").rearrange("p (t n) -> p t n", t=NT)
        cos_mla, sin_mla = rope_tab[:, :, 0:16], rope_tab[:, :, 16:32]
        cos_mb, sin_mb = rope_tab[:, :, 32:40], rope_tab[:, :, 40:48]
        ret_S0 = att[:, 0:1024].rearrange("p (h k) -> p h k", h=RET_H)
        ret_S1 = att[:, 1024:1536].rearrange("p (h k) -> p h k", h=RET_H)
        ret_V = att[:, 1536:1536 + 4096].rearrange("p (t n) -> p t n", t=NT)
        ret_O = proj[:, :, 0:2048]
        decay = mod_a[:, 0:1024].rearrange("p (h n) -> p h n", h=RET_H)
        gn_g = mod_a[:, 1024:3072]
        CW = NSA_G * N_CMP
        kv_shift = [att[:, at:at + 1024].rearrange("p (g s) -> p g s", g=NSA_G) for at in (0, 2560)]
        flat = [att[:, at:at + 16 * CW].rearrange("p (b n) -> p b n", b=16) for at in (1024, 3584)]
        flat_h, flat_l = ([y[:, 4 * w:4 * w + 4, :].rearrange("p k s -> p (k s)")[:, 0:16 * CW]
                           .rearrange("p (b n) -> p b n", b=16) for w in range(2)] for y in (yh, yl))
        cmp_hid = [att[0:CW, at:at + CMP_HID] for at in (2048, 4608)]
        cmp_hidT = [att[:, at:at + 2 * CW].rearrange("p (b n) -> p b n", b=2) for at in (2304, 4864)]
        cmp_w2 = mod_a[:, 0:256].rearrange("p (w b n) -> p w b n", w=2, b=2)
        pe_col = mod_a[:, 256:288].rearrange("p (w b) -> p w b", w=2)
        router = mod_a[:, 512:576].rearrange("p (k n) -> p k n", k=KB)
        nsa_gate = mod_a[:, 1024:1120].rearrange("p (t n) -> p t n", t=NT)
        kc = mod_a[0:HD, 1280:1280 + CW]
        vc = mod_a[0:N_CMP, 1408:1408 + NSA_G * HD]
        cmp_p = mod_a[:, 1792:2048]
        fac = mod_a[:, 2048:2064]
        cmp_pT = att[0:N_CMP, 3072:3072 + 2048].rearrange("p (t h q) -> p t h q", t=NT, h=NH)
        route = att[:, 2048:2560]
        logit = route[:, 0:16].rearrange("p (t e) -> p t e", t=NT)
        logitT = att[0:N_EXP, 5120:5120 + S]
        sel = route[:, 16:32].rearrange("p (t e) -> p t e", t=NT)
        place = route[:, 32:64].rearrange("p (t e) -> p t e", t=NT)
        gate = route[:, 64:80].rearrange("p (t e) -> p t e", t=NT)
        now = [route[:, 80:86], route[:, 86:92]]
        cmp_a = route[:, 128:256].rearrange("p (t e f) -> p t e f", t=NT, e=N_EXP)
        cmp_b = route[:, 256:384].rearrange("p (t e f) -> p t e f", t=NT, e=N_EXP)
        rt = route[:, 384:512]

        fill_of = [[(mod_b, i * 512, 0, 3 * D + i * 512) for i in range(4)],
                   [(mod_b, i * 512, 0, 3 * D + i * 512) for i in (4, 5)]
                   + [(mod_a, 2 * D + i * 512, 0, 2 * D + i * 512) for i in range(2)],
                   [(mod_a, i * 512, 1, i * 512) for i in range(4)]]

        def units_of(k_rows):
            return k_rows // (UROWS * P)

        def pe_program(pe, c):
            def clear(e):
                e.wait_ge(t_lo, c.at("t", 2))
                e.wait_ge(job_act, c.at("job_a", 1))
                e.wait_ge(job_dve, c.at("job_d", 1))

            def chunks_read(e):
                e.wait_ge(evac_act, c.at("chunk", 2))
                e.wait_ge(evac_dve, c.at("chunk", 2))

            def source(e):
                c.add("src")
                e.wait_ge(src_ready, c.at("src"))

            def unit(e, lhs, tiles, k0, banks, width, first, last, blocks=UROWS, at=0):
                slot, _ = c.slot()
                e.wait_ge(split_lo, c.at("unit", RING + 1))
                for t in range(tiles):
                    for j in range(blocks):
                        w = slice(j * USIZE // blocks, j * USIZE // blocks + width)
                        n = 0
                        for part, wp in ((lhs[0], whi), (lhs[0], wlo), (lhs[1], whi)):
                            mm = e.matmul(ps[0:lhs[2], banks[t], at:at + width], part[:, k0 + j, t * P:t * P + lhs[2]],
                                          wp[:, slot, w], start=first and j == 0 and n == 0,
                                          stop=last and j == blocks - 1 and n == 2)
                            n += 1
                mm.then_inc(unit_used, 1)
                c.add("unit")

            def chunk(e, lhs, tiles, rows, width=UCOLS):
                side = c.parity("chunk")
                e.wait_ge(evac_act, c.at("chunk", 1))
                e.wait_ge(evac_dve, c.at("chunk", 1))
                for i in range(units_of(rows)):
                    unit(e, lhs, tiles, i * UROWS, (2 * side, 2 * side + 1), width, i == 0,
                         i == units_of(rows) - 1)
                c.add("chunk")

            def turn_tiles(e, src, blocks):
                for t in range(NT):
                    source(e)
                    for b in range(0, blocks, 4):
                        bank = 6 + c.parity("t")
                        e.wait_ge(t_lo, c.at("t", 1))
                        for j in range(4):
                            tr = e.transpose(ps[:, bank, j * P:(j + 1) * P], src(t, b + j), ident)
                        tr.then_inc(t_ready, 1)
                        c.add("t")

            def turn(e, src, blocks, tiles=NT):
                for b in range(0, blocks, 2):
                    bank = 6 + c.parity("t")
                    e.wait_ge(t_lo, c.at("t", 1))
                    for j in range(2):
                        for t in range(tiles):
                            tr = e.transpose(ps[:, bank, (j * tiles + t) * P:(j * tiles + t + 1) * P],
                                             src(t, b + j), ident)
                    tr.then_inc(t_ready, 1)
                    c.add("t")

            def turned(e):
                e.wait_ge(t_lo, c.at("t", 2))

            def job(e, fill):
                side = c.parity("job")
                name, done = (("job_a", job_act), ("job_d", job_dve))[side]
                e.wait_ge(done, c.at(name, 1))
                fill(e, 6 + side).then_inc(job_ready, 1)
                c.add("job")
                c.add(name)

            def turns_of_heads(e, src, heads, d):
                for h in range(0, heads, 2):
                    def fill(e, bank):
                        e.sem_inc(pe_tick, 1)
                        for j in range(2):
                            for t in range(NT):
                                tr = e.transpose(ps[0:d, bank, (j * NT + t) * P:(j * NT + t + 1) * P],
                                                 src(t, h + j), ident)
                        return tr
                    job(e, fill)

            def fill_modulation(e, side):
                name, done = (("job_a", job_act), ("job_d", job_dve))[side]
                e.wait_ge(done, c.at(name, 1))
                for i in range(KB // UROWS):
                    unit(e, (chi, clo, P), 1, i * UROWS, (6 + side,), UCOLS, i == 0, i == KB // UROWS - 1)
                c.add(name)

            def softmax_heads(e, q, k, kheads, v, d, key, cmp=False, fill_in=False, new_q=True,
                              follows=False):
                if not follows:
                    source(e)
                clear(e)
                chunks_read(e)
                if new_q:
                    turns_of_heads(e, q, NH, d)
                turns_of_heads(e, k, kheads, d)
                if follows:
                    source(e)
                clear(e)

                def scores(g):
                    t, h0, n = HEAD_GROUPS[g]
                    for h in range(h0, h0 + n):
                        lo = h * P * (t + 1)
                        mm = e.matmul(ps[:, (0, 2)[t] + lo // 512, lo % 512:lo % 512 + P * (t + 1)],
                                      qT[0:d, h, t * P:(t + 1) * P], kT[0:d, key(h), 0:P * (t + 1)],
                                      start=True, stop=True)
                    mm.then_inc(score_ready, 1)

                def turns(g):
                    t, h0, n = HEAD_GROUPS[g]
                    c.add("prob")
                    e.wait_ge(prob_ready, c.at("prob"))
                    per = 4 // (t + 1)
                    for h in range(h0, h0 + n, per):
                        def fill(e, bank):
                            for j in range(per):
                                for b in range(t + 1):
                                    i = j * (t + 1) + b
                                    tr = e.transpose(ps[:, bank, i * P:(i + 1) * P],
                                                     prob[t][:, h + j, b * P:(b + 1) * P], ident)
                            return tr
                        job(e, fill)

                def outputs(g):
                    t, h0, n = HEAD_GROUPS[g]
                    clear(e)
                    for h in range(h0, h0 + n):
                        for b in range(t + 1):
                            mm = e.matmul(ps[:, t, h * HD:(h + 1) * HD], probT[:, h, t + b, :], v(b, h),
                                          start=b == 0, stop=b == t)
                    if h0 + n == NH:
                        mm.then_inc(pv_ready, 1)

                if cmp is not False:
                    cmp_scores(e, cmp)
                scores(0)
                scores(1)
                if fill_in:
                    fill_modulation(e, 0)
                if cmp is not False:
                    cmp_outputs(e, cmp)
                turns(0)
                scores(2)
                outputs(0)
                if fill_in:
                    fill_modulation(e, 1)
                turns(1)
                outputs(1)
                turns(2)
                outputs(2)
                if fill_in:
                    fill_modulation(e, 0)
                    fill_modulation(e, 1)
                    clear(e)

            def cmp_scores(e, s):
                for t in range(NT):
                    for h in range(NH):
                        g = (s * NH + h) // 4
                        mm = e.matmul(ps[:, 4, (t * NH + h) * N_CMP:(t * NH + h + 1) * N_CMP],
                                      qT[0:HD, h, t * P:(t + 1) * P], kc[:, g * N_CMP:(g + 1) * N_CMP],
                                      start=True, stop=True)
                mm.then_inc(score_ready, 1)

            def cmp_outputs(e, s):
                source(e)
                for t in range(NT):
                    for h0 in range(0, NH, 4):
                        def fill(e, bank):
                            for j in range(4):
                                n = (t * NH + h0 + j) * N_CMP
                                tr = e.transpose(ps[0:N_CMP, bank, j * P:(j + 1) * P], cmp_p[:, n:n + N_CMP], ident)
                            return tr
                        job(e, fill)
                clear(e)
                for t in range(NT):
                    for h in range(NH):
                        g = (s * NH + h) // 4
                        mm = e.matmul(ps[:, 4 + t, h * HD:(h + 1) * HD], cmp_pT[:, t, h, :],
                                      vc[:, g * HD:(g + 1) * HD], start=True, stop=True)
                mm.then_inc(pv_ready, 1)
                source(e)

            def stick_heads(e, q, k, v):
                source(e)
                clear(e)
                chunks_read(e)
                turns_of_heads(e, q, NH, HD)
                turns_of_heads(e, k, NH, HD)
                clear(e)
                for h in range(NH):
                    mm = e.matmul(ps[:, 2 + h // 2, (h % 2) * S:(h % 2 + 1) * S], kT[0:HD, h, 0:P],
                                  qT[0:HD, h, :], start=True, stop=True)
                for h in range(NH):
                    mm = e.matmul(ps[:, h // 4, (h % 4) * P:(h % 4 + 1) * P], kT[0:HD, h, P:S],
                                  qT[0:HD, h, P:S], start=True, stop=True)
                mm.then_inc(score_ready, 1)
                fill_modulation(e, 0)
                source(e)
                lk0 = kT[:, :, :]
                lk1 = qT[:, 0:4, :].rearrange("p a b -> p (a b)").rearrange("p (h k) -> p h k", h=NH)
                for b in range(4):
                    sums = ps[:, 2 + b, :].rearrange("p (h k) -> p h k", h=2)
                    pair = slice(2 * b, 2 * b + 2)
                    e.matmul(sums[:, :, 0:P], k_("later"), lk0[:, pair, 0:P], start=True, stop=True)
                    e.matmul(sums[:, :, P:S], k_("later"), lk0[:, pair, P:S], start=True, stop=False)
                    e.matmul(sums[:, :, P:S], k_("ones"), lk1[:, pair, :], start=False, stop=True)
                for b in range(2):
                    mm = e.matmul(ps[:, b, :], k_("later"), lk1[:, 4 * b:4 * b + 4, :], start=True, stop=True)
                mm.then_inc(score_ready, 1)
                fill_modulation(e, 1)
                fill_modulation(e, 0)
                c.add("prob")
                e.wait_ge(prob_ready, c.at("prob"))
                for h in range(NH):
                    e.matmul(ps[:, 0, h * HD:(h + 1) * HD], prob[1][:, h, 0:P], v(0, h), start=True, stop=True)
                for h in range(NH):
                    e.matmul(ps[:, 1, h * HD:(h + 1) * HD], prob[1][:, h, P:S], v(0, h), start=True, stop=False)
                    mm = e.matmul(ps[:, 1, h * HD:(h + 1) * HD], prob[0][:, h, :], v(1, h), start=False, stop=True)
                mm.then_inc(pv_ready, 1)
                fill_modulation(e, 1)
                clear(e)

            def step_in(e, lhs, kind, part, pieces={}):
                wide, _, _, tiles = kind
                if kind is SWIGLU:
                    for i in range(2):
                        unit(e, lhs, tiles, 4 * i, (0, 1), wide, i == 0, i == 1, 4, part * wide)
                elif kind is EXPERT:
                    for i in range(4):
                        unit(e, lhs, tiles, i * UROWS, (part,), UCOLS, i == 0, i == 3)
                        for piece in pieces.get(part * 4 + i, ()):
                            piece(e)
                else:
                    for i in (2 * part, 2 * part + 1):
                        unit(e, lhs, tiles, i * UROWS, (0, 1), UCOLS, i == 0, i == 3)

            def step_out(e, hid, kind, last=False):
                wide, _, _, tiles = kind
                for kg in range(wide // 256):
                    for n in range(2):
                        unit(e, hid, tiles, kg * UROWS, (2 + n * tiles, 3 + n * tiles), UCOLS, False,
                             last and kg == wide // 256 - 1)

            def turn_hidden(e, kind):
                e.wait_ge(evac_dve, c.at("chunk", 2))
                turn(e, lambda t, b: hidden[:, t, b * P:(b + 1) * P], kind[0] // P, kind[3])

            def clear_sums(e, kind, stop=False):
                for b in range(2 * kind[3]):
                    e.matmul(ps[:, 2 + b, :], zero[0:1, 0:P], zero[0:1, :], start=True, stop=stop)

            def step(e, lhs, hid, kind, pieces={}, last=False):
                chunks_read(e)
                step_in(e, lhs, kind, 0, pieces)
                turn_hidden(e, kind)
                step_in(e, lhs, kind, 1, pieces)
                c.add("chunk")
                turned(e)
                step_out(e, hid, kind, last)

            def mlp(e, lhs, hid, width, kind):
                wide, _, pair, tiles = kind
                steps = width // wide
                chunks_read(e)
                clear_sums(e, kind)
                step_in(e, lhs, kind, 0)
                step_in(e, lhs, kind, 1)
                c.add("chunk")

                def body(e, i):
                    for _ in range(pair):
                        step(e, lhs, hid, kind)
                loop(e, c, (steps - 1) // pair, body)
                for _ in range((steps - 1) % pair):
                    step(e, lhs, hid, kind)
                turn_hidden(e, kind)
                turned(e)
                step_out(e, hid, kind, last=True)

            def layer(e, l):
                for half in range(2):
                    turn_tiles(e, lambda t, b: work[:, t, b * P:(b + 1) * P], KB)
                    turned(e)
                    if half:
                        mlp(e, (xh, xl, P), (yh, yl, P), D_FF, RELU2)
                        break
                    X, Y = (xh, xl, P), (yh, yl, P)
                    chunk(e, X, NT, D)
                    chunk(e, X, NT, D)
                    chunk(e, X, NT, D, ROPE)
                    chunk(e, X, NT, D)
                    chunk(e, X, NT, D)
                    source(e)
                    turn(e, lambda t, b: proj[:, t, b * P:(b + 1) * P], 6)
                    turned(e)
                    chunk(e, Y, NT, Q_RANK)
                    chunk(e, Y, NT, Q_RANK, 256)
                    turn(e, lambda t, b: proj[:, t, Q_RANK + b * P:Q_RANK + (b + 1) * P], 2)
                    turned(e)
                    chunk(e, Y, NT, KV_RANK)
                    chunk(e, Y, NT, KV_RANK)
                    softmax_heads(e, lambda t, h: q_up[:, t, h * 96:(h + 1) * 96],
                                  lambda t, h: k_cat[:, t, h * 96:(h + 1) * 96], NH,
                                  lambda t, h: proj[:, t, h * P + HD:(h + 1) * P], MLA_QK, lambda h: h, fill_in=True)
                    for branch in range(3):
                        if branch:
                            for _ in range(5):
                                chunk(e, X, NT, D)
                            q = lambda t, h: proj[:, t, h * HD:(h + 1) * HD]
                            k = lambda t, h: proj[:, t, 512 + h * HD:512 + (h + 1) * HD]
                            v = lambda t, h: proj[:, t, 1024 + h * HD:1024 + (h + 1) * HD]
                            if branch == 1:
                                stick_heads(e, q, k, v)
                            else:
                                softmax_heads(e, q, k, NH, v, HD, lambda h: h, fill_in=True)
                        source(e)
                        turn(e, lambda t, b: heads_out[:, t, b * P:(b + 1) * P], 4)
                        turned(e)
                        chunk(e, Y, NT, 512)
                        chunk(e, Y, NT, 512)
                    source(e)
                    turn(e, lambda t, b: work[:, t, b * P:(b + 1) * P], KB)
                    turned(e)
                    chunk(e, Y, NT, D)
                    chunk(e, Y, NT, D)
                c.add("chunk")

            def retention(e):
                X, Y = (xh, xl, P), (yh, yl, P)
                turn_tiles(e, lambda t, b: x[:, t, b * P:(b + 1) * P], KB)
                turned(e)
                for _ in range(8):
                    chunk(e, X, NT, D)
                source(e)
                clear(e)
                for base in (0, D):
                    for b in range(0, KB, 2):
                        def fill(e, bank):
                            for j in range(2):
                                for t in range(NT):
                                    tr = e.transpose(ps[:, bank, (j * NT + t) * P:(j * NT + t + 1) * P],
                                                     proj[:, t, base + (b + j) * P:base + (b + j + 1) * P], ident)
                            return tr
                        job(e, fill)
                clear(e)
                chunks_read(e)
                for h in range(RET_H):
                    for b in range(2):
                        e.matmul(ps[:, 2 + h // 2, (h % 2) * S:(h % 2 + 1) * S], kT[:, 2 * h + b, 0:P],
                                 qT[:, 2 * h + b, :], start=b == 0, stop=b == 1)
                for h in range(RET_H):
                    for b in range(2):
                        mm = e.matmul(ps[:, 0, h * P:(h + 1) * P], kT[:, 2 * h + b, P:S],
                                      qT[:, 2 * h + b, P:S], start=b == 0, stop=b == 1)
                mm.then_inc(score_ready, 1)
                source(e)
                for h in range(RET_H):
                    def tile0(e, bank):
                        return e.matmul(ps[:, bank, :], ret_S0[:, h, 0:P], ret_V[:, 0, h * 512:(h + 1) * 512],
                                        start=True, stop=True)

                    def tile1(e, bank):
                        e.matmul(ps[:, bank, :], ret_S0[:, h, P:S], ret_V[:, 0, h * 512:(h + 1) * 512],
                                 start=True, stop=False)
                        return e.matmul(ps[:, bank, :], ret_S1[:, h, :], ret_V[:, 1, h * 512:(h + 1) * 512],
                                        start=False, stop=True)
                    job(e, tile0)
                    job(e, tile1)
                clear(e)
                for _ in range(4):
                    chunk(e, X, NT, D)
                chunks_read(e)
                for half in range(2):
                    source(e)
                    turn(e, lambda t, b: ret_O[:, t, half * D + b * P:half * D + (b + 1) * P], KB)
                    turned(e)
                    for kg in range(KB // UROWS):
                        for n in range(2):
                            unit(e, Y, NT, kg * UROWS, (2 + 2 * n, 3 + 2 * n), UCOLS,
                                 half == 0 and kg == 0, half == 1 and kg == KB // UROWS - 1)
                c.add("chunk")

            def swiglu_dense(e):
                turn_tiles(e, lambda t, b: x[:, t, b * P:(b + 1) * P], KB)
                turned(e)
                mlp(e, (xh, xl, P), (yh, yl, P), D_FF2, SWIGLU)
                c.add("chunk")

            def sparse_attention(e):
                turn_tiles(e, lambda t, b: x[:, t, b * P:(b + 1) * P], KB)
                turned(e)
                for _ in range(2):
                    chunk(e, (xh, xl, P), NT, D)
                chunk(e, (xh, xl, P), NT, D, 48)
                for _ in range(3):
                    chunk(e, (xh, xl, P), NT, D)
                for w in range(2):
                    source(e)
                    clear(e)
                    for g in range(0, NSA_G, 2):
                        def fill(e, bank):
                            for j in range(2):
                                for t in range(NT):
                                    at = w * 512 + (g + j) * P
                                    tr = e.transpose(ps[:, bank, (j * NT + t) * P:(j * NT + t + 1) * P],
                                                     work[:, t, at:at + P], ident)
                            return tr
                        job(e, fill)
                for w in range(2):
                    source(e)
                    side = c.parity("chunk")
                    e.wait_ge(evac_act, c.at("chunk", 1))
                    e.wait_ge(evac_dve, c.at("chunk", 1))
                    for i in range(16 // UROWS):
                        unit(e, (flat_h[w], flat_l[w], CW), 1, i * UROWS, (2 * side,), CMP_HID, i == 0,
                             i == 16 // UROWS - 1)
                    c.add("chunk")
                chunks_read(e)
                clear(e)
                for w in range(2):
                    def fill(e, bank):
                        for b in range(2):
                            tr = e.transpose(ps[:, bank, b * CW:(b + 1) * CW], cmp_hid[w][:, b * P:(b + 1) * P],
                                             ident[0:CW, 0:CW])
                        return tr
                    job(e, fill)
                clear(e)
                for w in range(2):
                    def fill(e, bank):
                        if w == 0:
                            for b in range(2):
                                mm = e.matmul(ps[0:HD, bank, 0:CW], cmp_w2[:, 0, b, :], cmp_hidT[w][:, b, :],
                                              start=b == 0, stop=b == 1)
                            return mm
                        for g in range(NSA_G):
                            for b in range(2):
                                mm = e.matmul(ps[0:N_CMP, bank, g * HD:(g + 1) * HD],
                                              cmp_hidT[w][:, b, g * N_CMP:(g + 1) * N_CMP], cmp_w2[:, 1, b, :],
                                              start=b == 0, stop=b == 1)
                        return mm
                    job(e, fill)
                clear(e)
                for s in range(2):
                    for kind in range(2):
                        softmax_heads(e, lambda t, h: proj[:, t, 1536 + (s * NH + h) * HD:1536 + (s * NH + h + 1) * HD],
                                      lambda t, g: proj[:, t, (2 + 2 * kind) * 256 + g * HD:(2 + 2 * kind) * 256 + (g + 1) * HD],
                                      NSA_G,
                                      lambda t, h: proj[:, t, (3 + 2 * kind) * 256 + (2 * s + h // 4) * HD:
                                                        (3 + 2 * kind) * 256 + (2 * s + h // 4 + 1) * HD],
                                      HD, lambda h: 2 * s + h // 4, s if kind == 0 else False, new_q=kind == 0,
                                      follows=s > 0 or kind > 0)
                source(e)
                turn(e, lambda t, b: work[:, t, b * P:(b + 1) * P], KB)
                turned(e)
                chunk(e, (yh, yl, P), NT, D)
                chunk(e, (yh, yl, P), NT, D)

            def experts(e):
                turn_tiles(e, lambda t, b: x[:, t, b * P:(b + 1) * P], KB)
                turned(e)
                clear(e)
                source(e)

                def fill(e, bank):
                    n = 0
                    for b in range(KB):
                        for part, r in ((xh, router_h), (xh, router_l), (xl, router_h)):
                            mm = e.matmul(ps[0:N_EXP, bank, 0:S], r[:, b, :], part[:, b, :],
                                          start=n == 0, stop=n == 3 * KB - 1)
                            n += 1
                    return mm
                job(e, fill)
                clear(e)
                for t in range(NT):
                    job(e, lambda e, bank: e.transpose(ps[:, bank, 0:N_EXP], logitT[:, t * P:(t + 1) * P],
                                                       ident[0:N_EXP, 0:N_EXP]))
                source(e)
                for t in range(NT):
                    def fill(e, bank):
                        e.matmul(ps[:, bank, 0:N_EXP], k_("earlier"), sel[:, t, :], start=True, stop=t == 0)
                        if t:
                            e.matmul(ps[:, bank, 0:N_EXP], k_("ones"), sel[:, 0, :], start=False, stop=True)
                        e.matmul(ps[:, bank, N_EXP:2 * N_EXP], k_("ones"), sel[:, 0, :], start=True, stop=False)
                        return e.matmul(ps[:, bank, N_EXP:2 * N_EXP], k_("ones"), sel[:, 1, :], start=False, stop=True)
                    job(e, fill)
                source(e)
                n_rounds = 1 if e is SILENT else e.value_load(rounds[0:1, 0:1], min_val=1, max_val=2)

                def gather(b):
                    def columns(half, part):
                        def fill(e, bank):
                            for j in range(4):
                                k = half * 4 + j
                                for t in range(NT):
                                    mm = e.matmul(ps[:, bank, j * P:(j + 1) * P], part[:, t, k * P:(k + 1) * P],
                                                  onehot[b][:, t, :], start=t == 0, stop=t == 1)
                            return mm
                        return lambda e: job(e, fill)

                    def rows(t):
                        return lambda e: job(e, lambda e, bank: e.transpose(ps[:, bank, 0:P],
                                                                            onehot[b][:, t, :].bitcast(F32), ident))
                    return [columns(half, part) for half in range(2) for part in (xth, xtl)] + [rows(t) for t in range(NT)]

                def scatter(b):
                    def part(t, n):
                        def piece(e):
                            if t == 0 and n == 0:
                                c.add("out")
                                e.wait_ge(out_lo, c.at("out"))
                            e.wait_ge(comb_free, c.at("comb", 1))
                            w = slice(n * 512, (n + 1) * 512)
                            e.matmul(ps[:, 4 + n, :], onehotT[b][:, t * P:(t + 1) * P], eh[:, w], start=True, stop=False)
                            e.matmul(ps[:, 4 + n, :], onehotT[b][:, t * P:(t + 1) * P], el[:, w], start=False,
                                     stop=True).then_inc(comb_ready, 1)
                            c.add("comb")
                        return piece
                    return [part(t, n) for t in range(NT) for n in range(2)]

                def one_expert(e, b, last=False):
                    now_, next_ = (tuple(gathered[b]) + (P,), tuple(gathered[1 - b]) + (P,))
                    hid = tuple(hidden_e) + (P,)
                    before = {4 + i: [piece] for i, piece in enumerate(scatter(1 - b))}
                    before[7].append(lambda e: clear_sums(e, EXPERT))
                    step(e, now_, hid, EXPERT, before)
                    if last:
                        step(e, now_, hid, EXPERT)
                    else:
                        job_of = gather(1 - b)
                        clear(e)
                        step(e, now_, hid, EXPERT, {0: [source, job_of[0], job_of[1]], 1: job_of[2:3],
                                                    2: job_of[3:4], 3: [clear], 5: [turned] + job_of[4:6], 7: [clear]})
                        e.sem_inc(pe_tick, 1)
                    loop(e, c, D_FFE // 512 - 3, lambda e, s: step(e, now_, hid, EXPERT))
                    if not last:
                        step(e, next_, hid, EXPERT, last=True)
                    else:
                        turn_hidden(e, EXPERT)
                        turned(e)
                        step_out(e, hid, EXPERT, last=True)

                def one_round(e, r):
                    clear_sums(e, EXPERT, stop=True)
                    source(e)
                    clear(e)
                    for piece in gather(0):
                        piece(e)
                    clear(e)
                    chunks_read(e)
                    step_in(e, tuple(gathered[0]) + (P,), EXPERT, 0)
                    step_in(e, tuple(gathered[0]) + (P,), EXPERT, 1)
                    c.add("chunk")

                    def two(e, i):
                        one_expert(e, 0)
                        one_expert(e, 1)
                    loop(e, c, N_EXP // 2 - 1, two)
                    one_expert(e, 0)
                    one_expert(e, 1, last=True)
                    for piece in scatter(1):
                        piece(e)
                loop(e, c, n_rounds, one_round)

            pe.wait_ge(const_ready, 16)
            pe.wait_ge(zero_ready, 1)
            pe.wait_ge(c_ready, 17)

            def two(e, i):
                chunk(e, (chi, clo, P), 1, D)
                chunk(e, (chi, clo, P), 1, D)
            loop(pe, c, 2, two)
            loop(pe, c, DEPTH, layer)
            retention(pe)
            swiglu_dense(pe)
            sparse_attention(pe)
            experts(pe)

        def act_program(act, c):
            def split(e, ahead):
                slot, turn_ = c.slot(ahead)
                e.wait_ge(raw_ready[slot], turn_ * 16 + 16)
                e.wait_ge(unit_used, c.at("unit", ahead + 1))
                e.activation(whi[:, slot, :], raw[:, slot, :], ACT.Copy).then_inc(split_hi, 1)

            def pass_units(e, n, pieces={}, first=0):
                for i in range(n):
                    split(e, LEAD)
                    c.add("unit")
                    for piece in pieces.get(first + i, ()):
                        piece(e)

            def chunk(e, rows, read=None):
                side = c.parity("chunk")
                pass_units(e, units_of(rows))
                c.add("chunk")
                if read is None:
                    e.wait_ge(evac_dve, c.at("chunk", 2))
                    e.sem_inc(evac_act, 1)
                    return
                e.wait_ge(unit_used, c.at("unit", RING))
                read(e, 2 * side).then_inc(evac_act, 1)

            def copy_to(dst):
                return lambda e, b: e.activation(dst, ps[:, b, 0:dst.shape[-1]], ACT.Copy)

            def sigmoid_to(dst):
                def read(e, b):
                    e.activation(dst[:, 0, :], ps[:, b, :], ACT.Sigmoid)
                    return e.activation(dst[:, 1, :], ps[:, b + 1, :], ACT.Sigmoid)
                return read

            def turn(e, hi, blocks, tiles=NT, by_tile=False):
                if by_tile:
                    for t, b in ((t, b) for t in range(NT) for b in range(0, blocks, 4)):
                        bank = 6 + c.parity("t")
                        c.add("t")
                        e.wait_ge(t_ready, c.at("t"))
                        e.activation(hi[:, b:b + 4, t * P:(t + 1) * P], ps[:, bank, :].rearrange("p (b s) -> p b s", b=4),
                                     ACT.Copy).then_inc(t_hi, 1)
                    return
                for b in range(0, blocks, 2):
                    bank = 6 + c.parity("t")
                    c.add("t")
                    e.wait_ge(t_ready, c.at("t"))
                    e.activation(hi[:, b:b + 2, :].rearrange("p b s -> p (b s)"), ps[:, bank, 0:2 * tiles * P],
                                 ACT.Copy).then_inc(t_hi, 1)

            def jobs(e, copies):
                for copy in copies:
                    side = c.parity("job")
                    c.add("job")
                    if side == 0:
                        e.wait_ge(job_ready, c.at("job"))
                        copy(e, 6).then_inc(job_act, 1)

            def plain(dst, src):
                return lambda e, bank: e.activation(dst, src(bank), ACT.Copy)

            def vec(e):
                c.add("vec")
                e.wait_ge(vec_ready, c.at("vec"))

            def root(e, n):
                vec(e)
                e.activation(st[:, 8:8 + n], st[:, 0:n], ACT.Sqrt).then_inc(act_ready, 1)

            def root_of_squares(e, sources):
                for i, v in enumerate(sources):
                    if i:
                        e.drain()
                    if i == 0 or len(sources) == NT:
                        vec(e)
                    e.activation(att[:, 5120:5120 + v.shape[-1]], v, ACT.Square, accum_out=st[:, i:i + 1])
                e.drain()
                for i in range(0, len(sources), NT):
                    r = e.activation(st[:, 8 + i:8 + i + NT], st[:, i:i + NT], ACT.Sqrt, bias=k_("eps"),
                                     scale=1.0 / sources[i].shape[-1])
                r.then_inc(act_ready, 1)

            def head_turns(dst, heads, d):
                return [plain(dst[0:d, h:h + 2, :], lambda bank: ps[0:d, bank, :].rearrange("p (h s) -> p h s", h=2))
                        for h in range(0, heads, 2)]

            def softmax_heads(e, kheads, d, cmp=False, fill_in=False, new_q=True):
                jobs(e, (head_turns(qT, NH, d) if new_q else []) + head_turns(kT, kheads, d))
                c.add("score", len(HEAD_GROUPS))

                def exponentials(g, units=0):
                    t, h0, n = HEAD_GROUPS[g]
                    vec(e)
                    for h in range(h0, h0 + n):
                        if h == h0 + n // 2:
                            pass_units(e, units)
                        ex = e.activation(prob[t][:, h, :], prob[t][:, h, :], ACT.Exp, bias=nmax[:, t * NH + h:t * NH + h + 1],
                                          accum_out=rsum[:, t * NH + h:t * NH + h + 1])
                    ex.then_inc(prob_ready, 1)

                if cmp is not False:
                    c.add("score")
                    vec(e)
                    e.activation(cmp_p[:, 0:240], cmp_p[:, 0:240], ACT.Exp).then_inc(act_ready, 1)
                if fill_in:
                    pass_units(e, 1)
                exponentials(0, 1 if fill_in else 0)
                if cmp is not False:
                    jobs(e, [plain(cmp_pT[:, t, h:h + 4, :],
                                   lambda bank: ps[0:N_CMP, bank, :].rearrange("p (h s) -> p h s", h=4))
                             for t in range(NT) for h in (0, 4)])
                exponentials(1)
                first, second = prob_turns(plain, 0, 4), prob_turns(plain, 1, 2)
                jobs(e, first)
                if fill_in:
                    pass_units(e, 3)
                exponentials(2)
                if fill_in:
                    pass_units(e, 1)
                jobs(e, second)
                if fill_in:
                    pass_units(e, 7)

            def stick_heads(e):
                jobs(e, head_turns(qT, NH, HD) + head_turns(kT, NH, HD))
                c.add("score")
                e.wait_ge(score_ready, c.at("score"))
                ab = (att[:, 1024:3072], att[:, 0:1024])
                z = (ps[:, 2:6, :].rearrange("p b n -> p (b n)"), ps[:, 0:2, :].rearrange("p b n -> p (b n)"))
                for b in range(2):
                    e.activation(ab[b], z[b], ACT.Abs, scale=0.125)
                e.drain().then_inc(act_ready, 1)
                for b in range(2):
                    e.activation(ab[b], ab[b], ACT.Exp, scale=-1.0)
                e.drain()
                pass_units(e, 1)
                e.activation(ab[0], ab[0], ACT.Ln, bias=1.0)
                e.activation(ab[1], ab[1], ACT.Ln, bias=1.0).then_inc(act_ready, 1)
                c.add("score")
                pass_units(e, 4)
                vec(e)
                e.activation(att[:, 0:3072], att[:, 3072:6144], ACT.Exp).then_inc(prob_ready, 1)
                pass_units(e, 8)

            def activate(e, kind):
                wide, tiles = kind[0], kind[3]
                e.wait_ge(unit_used, c.at("unit", RING))
                for t in range(tiles):
                    r = e.activation(act_tmp[:, t, 0:wide], ps[:, t, 0:wide], ACT.Relu if kind is RELU2 else ACT.Silu)
                r.then_inc(evac_act, 1)

            def step(e, hi, kind, pieces={}):
                n = kind[1] // 2
                pass_units(e, n, pieces)
                turn(e, hi, kind[0] // P, kind[3])
                pass_units(e, n, pieces, n)
                c.add("chunk")
                activate(e, kind)
                pass_units(e, kind[0] // P, pieces, 2 * n)

            def mlp(e, hi, width, kind):
                steps, pair = width // kind[0], kind[2]
                pass_units(e, kind[1])
                c.add("chunk")
                activate(e, kind)

                def body(e, i):
                    for _ in range(pair):
                        step(e, hi, kind)
                loop(e, c, (steps - 1) // pair, body)
                for _ in range((steps - 1) % pair):
                    step(e, hi, kind)
                turn(e, hi, kind[0] // P, kind[3])
                pass_units(e, kind[0] // P)
                c.add("chunk")

            def left_to_dve(e):
                e.wait_ge(evac_dve, c.at("chunk", 2))
                e.sem_inc(evac_act, 1)

            def layer(e, l):
                for half in range(2):
                    root_of_squares(e, [x[:, t, :] for t in range(NT)])
                    turn(e, xh, KB, by_tile=True)
                    if half:
                        mlp(e, yh, D_FF, RELU2)
                        left_to_dve(e)
                        break
                    chunk(e, D, copy_to(proj[:, 0, 0:512]))
                    chunk(e, D, copy_to(proj[:, 0, 512:1024]))
                    chunk(e, D, copy_to(proj[:, 0, 1024:1056]))
                    root_of_squares(e, [proj[:, 0, 0:768], proj[:, 1, 0:768], proj[:, 0, 768:1024], proj[:, 1, 768:1024]])
                    chunk(e, D, sigmoid_to(proj[:, :, 1536:2048]))
                    chunk(e, D, sigmoid_to(proj[:, :, 2048:2560]))
                    turn(e, yh, 6)
                    chunk(e, Q_RANK, copy_to(q_up[:, 0, 0:512]))
                    chunk(e, Q_RANK, copy_to(q_up[:, 0, 512:768]))
                    turn(e, yh, 2)
                    chunk(e, KV_RANK, copy_to(proj[:, 0, 0:512]))
                    chunk(e, KV_RANK, copy_to(proj[:, 0, 512:1024]))
                    softmax_heads(e, NH, MLA_QK, fill_in=True)
                    for branch in range(3):
                        if branch:
                            for i in range(3):
                                chunk(e, D, copy_to(proj[:, 0, i * 512:(i + 1) * 512]))
                            chunk(e, D, sigmoid_to(proj[:, :, 1536:2048]))
                            chunk(e, D, sigmoid_to(proj[:, :, 2048:2560]))
                            if branch == 1:
                                stick_heads(e)
                            else:
                                softmax_heads(e, NH, HD, fill_in=True)
                        turn(e, yh, 4)
                        pass_units(e, 3)
                        chunk(e, 512)
                        chunk(e, 512)
                    turn(e, yh, KB)
                    chunk(e, D)
                    chunk(e, D)

            def retention(e):
                turn(e, xh, KB, by_tile=True)
                for side in range(4):
                    chunk(e, D, copy_to(proj[:, 0, side * 512:side * 512 + 512]))
                for side in range(4):
                    chunk(e, D, copy_to(ret_V[:, 0, side * 512:side * 512 + 512]))
                jobs(e, [plain(dst[:, b:b + 2, :], lambda bank: ps[:, bank, :].rearrange("p (h s) -> p h s", h=2))
                         for dst in (qT, kT) for b in range(0, KB, 2)])
                jobs(e, [plain(ret_O[:, t, h * 512:(h + 1) * 512], lambda bank: ps[:, bank, :])
                         for h in range(RET_H) for t in range(NT)])
                vec(e)
                for side in range(4):
                    def read(e, b):
                        e.activation(ret_V[:, 0, side * 512:side * 512 + 512], ps[:, b, :], ACT.Silu)
                        return e.activation(ret_V[:, 1, side * 512:side * 512 + 512], ps[:, b + 1, :], ACT.Silu)
                    chunk(e, D, read)
                root(e, 8)
                for half in range(2):
                    turn(e, yh, KB)
                    pass_units(e, 8)
                c.add("chunk")
                left_to_dve(e)
                root(e, 2)

            def sparse_attention(e):
                turn(e, xh, KB, by_tile=True)
                for i in (3, 4):
                    chunk(e, D, copy_to(proj[:, 0, i * 512:(i + 1) * 512]))

                def gates(e, b):
                    e.activation(nsa_gate[:, 0, :], ps[:, b, 0:48], ACT.Sigmoid)
                    return e.activation(nsa_gate[:, 1, :], ps[:, b + 1, 0:48], ACT.Sigmoid)
                chunk(e, D, gates)
                for i in range(3):
                    chunk(e, D, copy_to(proj[:, 0, i * 512:(i + 1) * 512]))
                for w in range(2):
                    jobs(e, [shift_copy(w, 0), shift_copy(w, 2)])
                for w in range(2):
                    vec(e)
                    e.activation(flat_h[w], flat[w], ACT.Copy).then_inc(act_ready, 1)
                for w in range(2):
                    side = c.parity("chunk")
                    pass_units(e, 8)
                    c.add("chunk")
                    e.wait_ge(unit_used, c.at("unit", RING))
                    e.activation(cmp_hid[w], ps[0:CW, 2 * side, 0:CMP_HID], ACT.Gelu_apprx_tanh).then_inc(evac_act, 1)
                jobs(e, small_jobs(plain))
                for s in range(2):
                    for kind in range(2):
                        softmax_heads(e, NSA_G, HD, s if kind == 0 else False, new_q=kind == 0)
                turn(e, yh, KB)
                chunk(e, D)
                chunk(e, D)
                root(e, 2)

            def shift_copy(w, g):
                def copy(e, bank):
                    src = ps[:, bank, :].rearrange("p (g s) -> p g s", g=2)
                    e.activation(kv_shift[w][0:HD, g:g + 2, :], src[0:HD], ACT.Copy)
                    return e.activation(kv_shift[w][HD:P, g:g + 2, 0:S - 1], src[HD:P, :, 1:S], ACT.Copy)
                return copy

            def experts(e):
                turn(e, xh, KB, by_tile=True)
                vec(e)
                e.activation(router_h, router, ACT.Copy).then_inc(act_ready, 1)
                vec(e)
                e.activation(xth, x[:, :, :], ACT.Copy).then_inc(act_ready, 1)
                jobs(e, [plain(logitT, lambda bank: ps[0:N_EXP, bank, 0:S])]
                     + [plain(logit[:, t, :], lambda bank: ps[:, bank, 0:N_EXP]) for t in range(NT)])
                vec(e)
                e.activation(rt[:, 0:16], rt[:, 0:16], ACT.Exp).then_inc(act_ready, 1)
                jobs(e, [plain(place[:, t, :], lambda bank: ps[:, bank, 0:16]) for t in range(NT)])
                vec(e)
                n_rounds = 1 if e is SILENT else e.value_load(rounds[0:1, 0:1], min_val=1, max_val=2)

                def output(e):
                    e.wait_ge(unit_used, c.at("unit", RING))
                    e.activation(eh, ps[:, 2:4, :].rearrange("p b n -> p (b n)"), ACT.Copy).then_inc(out_hi, 1)

                def one_expert(e, b, last=False):
                    output(e)
                    step(e, hidden_e[0], EXPERT)
                    step(e, hidden_e[0], EXPERT, {} if last else gather_pieces(jobs, gather_jobs(plain, 1 - b)))
                    loop(e, c, D_FFE // 512 - 3, lambda e, s: step(e, hidden_e[0], EXPERT))
                    if not last:
                        step(e, hidden_e[0], EXPERT)
                    else:
                        turn(e, hidden_e[0], 4, 1)
                        pass_units(e, 4)

                def one_round(e, r):
                    jobs(e, gather_jobs(plain, 0))
                    pass_units(e, 8)
                    c.add("chunk")
                    activate(e, EXPERT)

                    def two(e, i):
                        one_expert(e, 0)
                        one_expert(e, 1)
                    loop(e, c, N_EXP // 2 - 1, two)
                    one_expert(e, 0)
                    one_expert(e, 1, last=True)
                    output(e)
                loop(e, c, n_rounds, one_round)

            act.wait_ge(c_ready, 16)
            act.activation(st[:, 16:24], st[:, 16:24], ACT.Silu).then_inc(act_ready, 1)
            vec(act)
            act.activation(st[:, 32:128], st[:, 32:128], ACT.Sin).then_inc(act_ready, 1)
            for u in range(LEAD):
                split(act, u)

            def two(e, i):
                chunk(e, D)
                chunk(e, D)
            loop(act, c, 2, two)
            loop(act, c, DEPTH, layer)
            root_of_squares(act, [x[:, t, :] for t in range(NT)])
            retention(act)
            turn(act, xh, KB, by_tile=True)
            mlp(act, yh, D_FF2, SWIGLU)
            left_to_dve(act)
            root(act, 2)
            sparse_attention(act)
            experts(act)
            act.wait_ge(vec_ready_last, 1)
            act.activation(st[:, 8:10], st[:, 0:2], ACT.Sqrt).then_inc(last_root, 1)

        def prob_turns(plain, t, per):
            out_ = []
            for h in range(0, NH, per):
                if t == 0:
                    out_.append(plain(probT[:, h:h + per, 0, :],
                                      lambda bank: ps[:, bank, :].rearrange("p (h s) -> p h s", h=4)))
                else:
                    out_.append(plain(probT[:, h:h + per, 1:3, :],
                                      lambda bank: ps[:, bank, :].rearrange("p (h b s) -> p h b s", h=2, b=2)))
            return out_

        def gather_pieces(jobs, copies):
            def of(n):
                return lambda e: jobs(e, copies[n:n + 1])
            return {0: [of(0)], 1: [of(1)], 2: [of(2)], 3: [of(3)], 6: [of(4)], 7: [of(5)]}

        def gather_jobs(plain, b):
            out_ = []
            for half in range(2):
                for part in range(2):
                    out_.append(plain(gathered[b][part][:, half * 4:half * 4 + 4, :],
                                      lambda bank: ps[:, bank, :].rearrange("p (k s) -> p k s", k=4)))
            for t in range(NT):
                out_.append(plain(onehotT[b][:, t * P:(t + 1) * P], lambda bank: ps[:, bank, 0:P]))
            return out_

        def small_jobs(plain):
            return ([plain(cmp_hidT[w], lambda bank: ps[:, bank, 0:2 * CW].rearrange("p (b n) -> p b n", b=2))
                     for w in range(2)]
                    + [plain(kc, lambda bank: ps[0:HD, bank, 0:CW]),
                       plain(vc, lambda bank: ps[0:N_CMP, bank, 0:NSA_G * HD])])

        vec_ready_last, last_root = sem("vec_ready_last"), sem("last_root")

        def dve_program(dve, c):
            def split(e, ahead):
                slot, _ = c.slot(ahead)
                e.wait_ge(split_hi, c.at("unit", ahead + 1))
                e.tensor_tensor(wlo[:, slot, :], raw[:, slot, :], whi[:, slot, :].bitcast(F32),
                                ALU.subtract).then_inc(split_lo, 1)

            def pass_units(e, n, pieces={}, first=0):
                for i in range(n):
                    split(e, LEAD)
                    c.add("unit")
                    for piece in pieces.get(first + i, ()):
                        piece(e)

            def chunk(e, rows, read=None, pieces=()):
                side = c.parity("chunk")
                pass_units(e, units_of(rows), {i: [piece] for i, piece in enumerate(pieces)})
                c.add("chunk")
                if read is None:
                    e.wait_ge(evac_act, c.at("chunk", 2))
                    e.sem_inc(evac_dve, 1)
                    return
                e.wait_ge(unit_used, c.at("unit", RING))
                read(e, 2 * side).then_inc(evac_dve, 1)

            def copy_to(dst):
                return lambda e, b: e.tensor_copy(dst, ps[:, b + 1, 0:dst.shape[-1]])

            def turn(e, hi, lo, blocks, tiles=NT, by_tile=False):
                if by_tile:
                    for t, b in ((t, b) for t in range(NT) for b in range(0, blocks, 4)):
                        bank = 6 + c.parity("t")
                        c.add("t")
                        e.wait_ge(t_hi, c.at("t"))
                        w = (slice(None), slice(b, b + 4), slice(t * P, (t + 1) * P))
                        e.tensor_tensor(lo[w], ps[:, bank, :].rearrange("p (b s) -> p b s", b=4),
                                        hi[w].bitcast(F32), ALU.subtract).then_inc(t_lo, 1)
                    return
                for b in range(0, blocks, 2):
                    bank = 6 + c.parity("t")
                    c.add("t")
                    e.wait_ge(t_hi, c.at("t"))
                    e.tensor_tensor(lo[:, b:b + 2, :].rearrange("p b s -> p (b s)"), ps[:, bank, 0:2 * tiles * P],
                                    hi[:, b:b + 2, :].rearrange("p b s -> p (b s)").bitcast(F32),
                                    ALU.subtract).then_inc(t_lo, 1)

            def jobs(e, copies):
                for copy in copies:
                    side = c.parity("job")
                    c.add("job")
                    if side == 0:
                        c.add("job_a")
                    if side == 1:
                        e.wait_ge(job_ready, c.at("job"))
                        copy(e, 7).then_inc(job_dve, 1)

            def plain(dst, src):
                return lambda e, bank: e.tensor_copy(dst, src(bank))

            def to_act(e):
                e.drain().then_inc(vec_ready, 1)

            def from_act(e):
                c.add("act")
                e.wait_ge(act_ready, c.at("act"))

            def to_pe(e):
                e.drain().then_inc(src_ready, 1)

            def chunks_read_by_act(e):
                e.drain()
                e.wait_ge(evac_act, c.at("chunk", 2))

            def take_modulation(e, branch, n, passed):
                buf, at, _, _ = fill_of[branch][n]
                region = 2 if buf is mod_b else (0 if at < 2 * D else 1)
                side = n % 2
                e.wait_ge(bias_ready[region], biases(region))
                e.wait_ge(unit_used, c.at("unit", RING + 4 - passed))
                e.tensor_tensor(buf[:, at:at + 512], ps[:, 6 + side, :], buf[:, at:at + 512],
                                ALU.add).then_inc((job_act, job_dve)[side], 1)
                if side == 0:
                    c.add("job_a")

            def biases(region):
                return c.at(f"bias{region}") * 16

            def inverse_root(e, n):
                from_act(e)
                e.reciprocal(st[:, 16:16 + n], st[:, 8:8 + n])
                e.drain()

            def take_gain(e, which, loads=1):
                name, ready = (("ga", gain_a_ready), ("gb", gain_b_ready))[which]
                c.add(name, loads)
                e.wait_ge(ready, c.at(name) * 16)

            def scale_gain(e, mod):
                take_gain(e, 0)
                e.scalar_tensor_tensor(mod[:, D:2 * D], mod[:, D:2 * D], 1.0, gain_a[:, :], ALU.add, ALU.mult)
                e.drain().then_inc(gain_a_used, 1)

            def modulated_norm(e, mod):
                for t in range(NT):
                    e.tensor_tensor(work[:, t, :], x[:, t, :], mod[:, D:2 * D], ALU.mult)
                inverse_root(e, NT)
                for t in range(NT):
                    e.scalar_tensor_tensor(work[:, t, :], work[:, t, :], st[:, 16 + t:17 + t], mod[:, 0:D],
                                           ALU.mult, ALU.add)
                    to_pe(e)

            def rope(e, x1, x2, cos, sin, t1, t2):
                e.tensor_tensor(t1, x1, sin, ALU.mult)
                e.tensor_tensor(t2, x2, sin, ALU.mult)
                e.drain()
                e.tensor_tensor(x1, x1, cos, ALU.mult)
                e.tensor_tensor(x2, x2, cos, ALU.mult)
                e.drain()
                e.tensor_tensor(x1, x1, t2, ALU.subtract)
                e.tensor_tensor(x2, x2, t1, ALU.add)
                e.drain()

            def rope_heads(e, src, heads, half, cos, sin, at):
                shape = [P, heads, half]
                n = heads * half
                t1, t2 = (att[:, at + i * n:at + (i + 1) * n].rearrange("p (h d) -> p h d", h=heads) for i in range(2))
                rope(e, src[:, :, 0:half], src[:, :, half:2 * half],
                     cos.rearrange("p (o d) -> p o d", o=1).broadcast_to(shape),
                     sin.rearrange("p (o d) -> p o d", o=1).broadcast_to(shape), t1, t2)

            def over_heads(v, heads, n):
                return v.rearrange("p (h o) -> p h o", o=1).broadcast_to([P, heads, n])

            def row_over_heads(v, heads):
                return v.rearrange("p (o n) -> p o n", o=1).broadcast_to([P, heads, v.shape[-1]])

            def head_turns(dst, heads, d):
                return [plain(dst[0:d, h:h + 2, :], lambda bank: ps[0:d, bank, :].rearrange("p (h s) -> p h s", h=2))
                        for h in range(0, heads, 2)]

            def softmax_heads(e, kheads, d, scale, write, cmp=False, branch=None, new_q=True):
                filled = branch is not None
                jobs(e, (head_turns(qT, NH, d) if new_q else []) + head_turns(kT, kheads, d))

                def masked_scores(g):
                    t, h0, n = HEAD_GROUPS[g]
                    c.add("score")
                    e.wait_ge(score_ready, c.at("score"))
                    first = (0, 2)[t] + h0 * P * (t + 1) // 512
                    sc = ps[:, first:first + 2, :].rearrange("p b n -> p (b n)").rearrange("p (h k) -> p h k", h=n)
                    mask = k_("causal")[:, P:2 * P] if t == 0 else k_("causal")
                    top = nmax[:, t * NH + h0:t * NH + h0 + n]
                    e.scalar_tensor_tensor(prob[t][:, h0:h0 + n, :], sc, scale, row_over_heads(mask, n), ALU.mult, ALU.add)
                    e.drain()
                    e.tensor_reduce(top, prob[t][:, h0:h0 + n, :], AX, ALU.max)
                    e.drain()
                    e.tensor_scalar(top, top, -1.0, None, ALU.mult)
                    to_act(e)

                def output(t):
                    c.add("pv")
                    e.wait_ge(pv_ready, c.at("pv"))
                    e.reciprocal(rsum[:, t * NH:(t + 1) * NH], rsum[:, t * NH:(t + 1) * NH])
                    e.drain()
                    write(e, t, ps[:, t, :].rearrange("p (h d) -> p h d", h=NH))

                if cmp is not False:
                    cmp_softmax(e, cmp)
                masked_scores(0)
                if filled:
                    pass_units(e, 2)
                masked_scores(1)
                if filled:
                    take_modulation(e, branch, 0, 2)
                if cmp is not False:
                    cmp_output(e, cmp)
                jobs(e, prob_turns(plain, 0, 4))
                if filled:
                    pass_units(e, 3)
                masked_scores(2)
                output(0)
                if filled:
                    pass_units(e, 1)
                    take_modulation(e, branch, 1, 2)
                jobs(e, prob_turns(plain, 1, 2))
                output(1)
                if filled:
                    to_pe(e)
                    pass_units(e, 5)
                    take_modulation(e, branch, 2, 3)
                    pass_units(e, 2)
                    take_modulation(e, branch, 3, 1)

            def normed(e, t, o):
                e.tensor_tensor(heads_out[:, t, :].rearrange("p (h d) -> p h d", h=NH), o,
                                over_heads(rsum[:, t * NH:(t + 1) * NH], NH, HD), ALU.mult)

            def stick_heads(e):
                jobs(e, head_turns(qT, NH, HD) + head_turns(kT, NH, HD))
                c.add("score")
                e.wait_ge(score_ready, c.at("score"))
                z = (ps[:, 2:6, :].rearrange("p b n -> p (b n)"), ps[:, 0:2, :].rearrange("p b n -> p (b n)"))
                log_beta = (att[:, 4096:6144], att[:, 3072:4096])
                soft = (att[:, 1024:3072], att[:, 0:1024])
                keep = (kT[:, :, :].rearrange("p a b -> p (a b)"), qT[:, 0:4, :].rearrange("p a b -> p (a b)"))
                from_act(e)
                for b in range(2):
                    e.tensor_scalar(log_beta[b], z[b], 0.125, 0.0, ALU.mult, ALU.min)
                e.drain()
                for b in range(2):
                    e.scalar_tensor_tensor(keep[b], z[b], -0.125, log_beta[b], ALU.mult, ALU.add)
                pass_units(e, 1)
                e.drain()
                from_act(e)
                for b in range(2):
                    e.tensor_tensor(keep[b], keep[b], soft[b], ALU.subtract)
                e.drain()
                past, not_past = row_over_heads(k_("earlier"), NH), row_over_heads(k_("not_earlier"), NH)
                k0 = keep[0].rearrange("p (h k) -> p h k", h=NH)[:, :, 0:P]
                k1 = keep[1].rearrange("p (h k) -> p h k", h=NH)
                e.tensor_tensor(k0, k0, past, ALU.mult)
                e.tensor_tensor(k1, k1, past, ALU.mult)
                to_pe(e)
                for b in range(2):
                    e.tensor_tensor(log_beta[b], log_beta[b], soft[b], ALU.subtract)
                take_modulation(e, 1, 0, 1)
                e.drain()
                b0 = log_beta[0].rearrange("p (h k) -> p h k", h=NH)[:, :, 0:P]
                b1 = log_beta[1].rearrange("p (h k) -> p h k", h=NH)
                e.tensor_tensor(b0, b0, not_past, ALU.add)
                e.tensor_tensor(b1, b1, not_past, ALU.add)
                pass_units(e, 3)
                e.drain()
                c.add("score")
                e.wait_ge(score_ready, c.at("score"))
                for b in range(2):
                    e.tensor_tensor(log_beta[b], log_beta[b], z[b], ALU.add)
                to_act(e)
                pass_units(e, 6)
                take_modulation(e, 1, 1, 6)
                take_modulation(e, 1, 2, 2)
                c.add("pv")
                e.wait_ge(pv_ready, c.at("pv"))
                e.tensor_copy(heads_out, ps[:, 0:2, :])
                to_pe(e)
                pass_units(e, 3)
                take_modulation(e, 1, 3, 1)

            def make_hidden(e, kind):
                wide, tiles = kind[0], kind[3]
                e.wait_ge(evac_act, c.at("chunk", 2))
                for t in range(tiles):
                    other = act_tmp[:, t, :] if kind is RELU2 else ps[:, 1, :]
                    if kind is SWIGLU:
                        other = ps[:, t, wide:2 * wide]
                    r = e.tensor_tensor(hidden[:, t, 0:wide], act_tmp[:, t, 0:wide], other, ALU.mult)
                r.then_inc(evac_dve, 1)

            def step(e, hid, kind, pieces={}):
                n = kind[1] // 2
                pass_units(e, n, pieces)
                turn(e, hid[0], hid[1], kind[0] // P, kind[3])
                pass_units(e, n, pieces, n)
                c.add("chunk")
                make_hidden(e, kind)
                pass_units(e, kind[0] // P, pieces, 2 * n)

            def mlp(e, hid, width, kind):
                steps, pair = width // kind[0], kind[2]
                pass_units(e, kind[1])
                c.add("chunk")
                make_hidden(e, kind)

                def body(e, i):
                    for _ in range(pair):
                        step(e, hid, kind)
                loop(e, c, (steps - 1) // pair, body)
                for _ in range((steps - 1) % pair):
                    step(e, hid, kind)
                turn(e, hid[0], hid[1], kind[0] // P, kind[3])
                pass_units(e, kind[0] // P)
                c.add("chunk")

            def layer(e, l):
                for half in range(2):
                    mod = (mod_a, mod_b)[half]
                    if half == 0:
                        scale_gain(e, mod)
                    modulated_norm(e, mod)
                    if half == 0:
                        e.sem_inc(bias_used[0], 1)
                        for region in range(3):
                            c.add(f"bias{region}")
                    turn(e, xh, xl, KB, by_tile=True)
                    if half:
                        mlp(e, (yh, yl), D_FF, RELU2)

                        def gated(t, n):
                            e.tensor_tensor(work[:, t, n * 512:(n + 1) * 512], ps[:, 2 + 2 * n + t, :],
                                            mod[:, 2 * D + n * 512:2 * D + (n + 1) * 512], ALU.mult)
                        e.wait_ge(unit_used, c.at("unit", RING - 1))
                        for t in range(NT):
                            gated(t, 0)
                        e.wait_ge(unit_used, c.at("unit", RING))
                        for t in range(NT):
                            gated(t, 1)
                            e.drain()
                            if t == NT - 1:
                                e.sem_inc(evac_dve, 1)
                                e.sem_inc(bias_used[2], 1)
                            e.tensor_tensor(x[:, t, :], x[:, t, :], work[:, t, :], ALU.add)
                            to_act(e)
                        break
                    chunk(e, D, copy_to(proj[:, 1, 0:512]))
                    chunk(e, D, copy_to(proj[:, 1, 512:1024]))
                    chunk(e, D, copy_to(proj[:, 1, 1024:1056]))
                    chunks_read_by_act(e)
                    e.sem_inc(vec_ready, 1)
                    inverse_root(e, 4)
                    take_gain(e, 1, 2)
                    for t in range(NT):
                        e.scalar_tensor_tensor(proj[:, t, 0:768], proj[:, t, 0:768], st[:, 16 + t:17 + t],
                                               gain_b[:, 0:768], ALU.mult, ALU.mult)
                        e.scalar_tensor_tensor(proj[:, t, 768:1024], proj[:, t, 768:1024], st[:, 18 + t:19 + t],
                                               gain_b[:, 768:1024], ALU.mult, ALU.mult)
                    e.drain().then_inc(gain_b_used, 1)

                    def shared_key(t):
                        def piece(e):
                            rope_heads(e, proj[:, t, 1024:1056].rearrange("p (h d) -> p h d", h=1), 1, 16,
                                       cos_mla[:, t, :], sin_mla[:, t, :], 4608)
                            kt = k_cat[:, t, :].rearrange("p (h d) -> p h d", h=NH)
                            e.tensor_copy(kt[:, :, HD:MLA_QK], row_over_heads(proj[:, t, 1024:1056], NH))
                        return piece

                    def query_rope(t):
                        def piece(e):
                            if t == 0:
                                chunks_read_by_act(e)
                            rope_heads(e, q_up[:, t, :].rearrange("p (h d) -> p h d", h=NH)[:, :, HD:MLA_QK], NH, 16,
                                       cos_mla[:, t, :], sin_mla[:, t, :], 4608)
                        return piece
                    to_pe(e)
                    chunk(e, D)
                    chunk(e, D, None, [shared_key(t) for t in range(NT)])
                    turn(e, yh, yl, 6)
                    chunk(e, Q_RANK, copy_to(q_up[:, 1, 0:512]))
                    chunk(e, Q_RANK, copy_to(q_up[:, 1, 512:768]))
                    turn(e, yh, yl, 2)
                    chunk(e, KV_RANK, copy_to(proj[:, 1, 0:512]), [query_rope(0)])
                    chunk(e, KV_RANK, copy_to(proj[:, 1, 512:1024]), [query_rope(1)])
                    chunks_read_by_act(e)
                    for t in range(NT):
                        kt = k_cat[:, t, :].rearrange("p (h d) -> p h d", h=NH)
                        e.tensor_copy(kt[:, :, 0:HD], proj[:, t, 0:1024].rearrange("p (h d) -> p h d", h=NH)[:, :, 0:HD])
                    to_pe(e)
                    softmax_heads(e, NH, MLA_QK, float(1.0 / np.sqrt(MLA_QK)), normed, branch=0)
                    for branch in range(3):
                        if branch:
                            def key_rope(t):
                                def piece(e):
                                    if t == 0:
                                        chunks_read_by_act(e)
                                    rope_heads(e, proj[:, t, 0:1024].rearrange("p (h d) -> p h d", h=2 * NH), 2 * NH, 8,
                                               cos_mb[:, t, :], sin_mb[:, t, :], 4608)
                                return piece
                            for i in range(3):
                                chunk(e, D, copy_to(proj[:, 1, i * 512:(i + 1) * 512]))
                            chunk(e, D, None, [key_rope(t) for t in range(NT)] if branch == 2 else ())
                            chunk(e, D)
                            if branch == 1:
                                to_pe(e)
                                stick_heads(e)
                            else:
                                to_pe(e)
                                softmax_heads(e, NH, HD, 0.125, normed, branch=2)
                        turn(e, yh, yl, 4)
                        pass_units(e, 3)
                        for n in range(2):
                            def read(e, b):
                                dst = work[:, :, n * 512:(n + 1) * 512]
                                g = proj[:, :, 1536 + n * 512:2048 + n * 512]
                                if branch == 0:
                                    return e.tensor_tensor(dst, ps[:, b:b + 2, :], g, ALU.mult)
                                tmp = att[:, n * 1024:(n + 1) * 1024].rearrange("p (t n) -> p t n", t=NT)
                                e.tensor_tensor(tmp, ps[:, b:b + 2, :], g, ALU.mult)
                                e.drain()
                                return e.tensor_tensor(dst, dst, tmp, ALU.add)
                            chunk(e, 512, read)
                        e.drain()
                        if branch == 1:
                            scale_gain(e, mod_b)
                    to_pe(e)
                    turn(e, yh, yl, KB)
                    for n in range(2):
                        def read(e, b):
                            tmp = att[:, n * 1024:(n + 1) * 1024].rearrange("p (t n) -> p t n", t=NT)
                            w = slice(n * 512, (n + 1) * 512)
                            for t in range(NT):
                                e.tensor_tensor(tmp[:, t, :], ps[:, b + t, :], mod[:, 2 * D + n * 512:2 * D + (n + 1) * 512],
                                                ALU.mult)
                            e.drain()
                            return e.tensor_tensor(x[:, :, w], x[:, :, w], tmp, ALU.add)
                        chunk(e, D, read)
                    for _ in range(NT):
                        to_act(e)
                    e.sem_inc(bias_used[1], 1)

            def rms_final(e):
                take_gain(e, 0)
                inverse_root(e, NT)
                for t in range(NT):
                    e.scalar_tensor_tensor(x[:, t, :], x[:, t, :], st[:, 16 + t:17 + t], gain_a[:, :], ALU.mult, ALU.mult)
                    to_pe(e)
                e.sem_inc(gain_a_used, 1)

            def inverse_deviation(e, n, final=False):
                mv = st[:, 64:64 + 2 * n].rearrange("p (i k) -> p i k", k=2)
                e.tensor_scalar(st[:, 0:n], mv[:, :, 1], LN_EPS, None, ALU.add)
                if final:
                    e.drain().then_inc(vec_ready_last, 1)
                    e.wait_ge(last_root, 1)
                else:
                    to_act(e)
                    from_act(e)
                e.reciprocal(st[:, 16:16 + n], st[:, 8:8 + n])
                e.drain()

            def half_moments(e, h):
                e.drain()
                for t in range(NT):
                    e.bn_stats(st[:, 32 + 12 * t + 6 * h:38 + 12 * t + 6 * h], x[:, t, h * 512:(h + 1) * 512])

            def layer_norm(e, final=False):
                half_moments(e, 1)
                e.drain()
                for t in range(NT):
                    e.bn_aggr(st[:, 64 + 2 * t:66 + 2 * t], st[:, 32 + 12 * t:44 + 12 * t])
                e.drain()
                inverse_deviation(e, NT, final)
                if final:
                    e.wait_ge(last_gain, 32)
                else:
                    take_gain(e, 0)
                    take_gain(e, 1)
                for t in range(NT):
                    e.scalar_tensor_tensor(x[:, t, :], x[:, t, :], st[:, 64 + 2 * t:65 + 2 * t], gain_a[:, :],
                                           ALU.subtract, ALU.mult)
                    e.drain()
                    e.scalar_tensor_tensor(x[:, t, :], x[:, t, :], st[:, 16 + t:17 + t], gain_b[:, :], ALU.mult, ALU.add)
                    to_pe(e)
                e.sem_inc(gain_a_used, 1)
                e.sem_inc(gain_b_used, 1)

            def add_mlp(e):
                for n in range(2):
                    if n:
                        half_moments(e, 0)
                    e.wait_ge(unit_used, c.at("unit", RING - 1 + n))
                    w = slice(n * 512, (n + 1) * 512)
                    for t in range(NT):
                        e.scalar_tensor_tensor(x[:, t, w], x[:, t, w], ALPHA, ps[:, 2 + 2 * n + t, :], ALU.mult, ALU.add)
                e.drain().then_inc(evac_dve, 1)

            def retention(e):
                turn(e, xh, xl, KB, by_tile=True)

                def rope_head(base, t, h):
                    def piece(e):
                        if t == 0 and h == 0:
                            chunks_read_by_act(e)
                        at = base + h * RET_DK
                        rope_heads(e, proj[:, t, at:at + RET_DK].rearrange("p (h d) -> p h d", h=1), 1, P,
                                   k_("ret_cos")[:, t * P:(t + 1) * P], k_("ret_sin")[:, t * P:(t + 1) * P], 0)
                    return piece

                def copy(dst):
                    return lambda e, b: e.tensor_copy(dst, ps[:, b + 1, :])
                for side in range(2):
                    chunk(e, D, copy(proj[:, 1, side * 512:side * 512 + 512]))
                for side in range(2):
                    chunk(e, D, copy(proj[:, 1, D + side * 512:D + side * 512 + 512]),
                          [rope_head(0, side, h) for h in range(RET_H)])
                for side in range(4):
                    chunk(e, D, copy(ret_V[:, 1, side * 512:side * 512 + 512]),
                          [rope_head(D, side, h) for h in range(RET_H)] if side < 2 else ())
                    if side == 1:
                        to_pe(e)
                jobs(e, [plain(dst[:, b:b + 2, :], lambda bank: ps[:, bank, :].rearrange("p (h s) -> p h s", h=2))
                         for dst in (qT, kT) for b in range(0, KB, 2)])
                c.add("score")
                e.wait_ge(score_ready, c.at("score"))
                e.wait_ge(extra_ready, 32)
                s0 = ps[:, 2:4, :].rearrange("p b n -> p (b n)").rearrange("p (h k) -> p h k", h=RET_H)
                e.scalar_tensor_tensor(ret_S0, s0, 1.0 / 16, decay, ALU.mult, ALU.mult)
                e.scalar_tensor_tensor(ret_S1, ps[:, 0, :].rearrange("p (h k) -> p h k", h=RET_H), 1.0 / 16,
                                       decay[:, :, 0:P], ALU.mult, ALU.mult)
                chunks_read_by_act(e)
                to_pe(e)
                jobs(e, [plain(ret_O[:, t, h * 512:(h + 1) * 512], lambda bank: ps[:, bank, :])
                         for h in range(RET_H) for t in range(NT)])
                act_copied(e)
                to_act(e)

                def view(t, h):
                    return ret_O[:, t, h * 512:(h + 1) * 512]

                def moments(t, h):
                    def piece(e):
                        i = t * RET_H + h
                        e.bn_stats(st[:, 32:38], view(t, h))
                        e.drain()
                        e.bn_aggr(st[:, 64 + 2 * i:66 + 2 * i], st[:, 32:38])
                        e.drain()
                        e.scalar_tensor_tensor(view(t, h), view(t, h), st[:, 64 + 2 * i:65 + 2 * i],
                                               gn_g[:, h * 512:(h + 1) * 512], ALU.subtract, ALU.mult)
                    return piece
                for side in range(4):
                    chunk(e, D, None, [moments(side // 2, side % 2 * 2 + h) for h in range(2)])
                e.drain()
                inverse_deviation(e, 8)
                chunks_read_by_act(e)
                for h in range(RET_H):
                    for t in range(NT):
                        i = t * RET_H + h
                        e.scalar_tensor_tensor(view(t, h), view(t, h), st[:, 16 + i:17 + i], ret_V[:, t, h * 512:(h + 1) * 512],
                                               ALU.mult, ALU.mult)
                    if h % 2:
                        to_pe(e)
                for half in range(2):
                    turn(e, yh, yl, KB)
                    pass_units(e, 8)
                c.add("chunk")
                e.drain().then_inc(extra_used, 1)
                add_mlp(e)
                layer_norm(e)

            def act_copied(e):
                e.drain()
                e.wait_ge(job_act, c.at("job_a", 1))

            def shift_copy(w, g):
                def copy(e, bank):
                    src = ps[:, bank, :].rearrange("p (g s) -> p g s", g=2)
                    e.tensor_copy(kv_shift[w][0:HD, g:g + 2, :], src[0:HD])
                    return e.tensor_copy(kv_shift[w][HD:P, g:g + 2, 0:S - 1], src[HD:P, :, 1:S])
                return copy

            def sparse_attention(e):
                turn(e, xh, xl, KB, by_tile=True)

                def rope_piece(t, at, heads, wait=False):
                    def piece(e):
                        if wait:
                            chunks_read_by_act(e)
                        cos, sin = (k_(n)[:, t * 32:(t + 1) * 32] for n in ("nsa_cos", "nsa_sin"))
                        rope_heads(e, proj[:, t, at:at + heads * HD].rearrange("p (h d) -> p h d", h=heads), heads, 32,
                                   cos, sin, 5120)
                    return piece
                for i in (3, 4):
                    chunk(e, D, copy_to(proj[:, 1, i * 512:(i + 1) * 512]))
                chunk(e, D)
                for i in range(3):
                    if i < 2:
                        pieces = [rope_piece(i, 1536 + j * 256, 4, j == 0) for j in range(4)]
                    else:
                        pieces = [rope_piece(0, 0, 4, True), rope_piece(1, 0, 4), rope_piece(0, 512, 4), rope_piece(1, 512, 4)]
                    chunk(e, D, copy_to(proj[:, 1, i * 512:(i + 1) * 512]), pieces)
                e.wait_ge(extra_small, 80)
                for w in range(2):
                    for t in range(NT):
                        src = proj[:, t, w * 256:(w + 1) * 256].rearrange("p (g d) -> p g d", g=NSA_G)
                        dst = work[:, t, w * 512:(w + 1) * 512].rearrange("p (g r d) -> p g r d", g=NSA_G, r=2)
                        e.tensor_copy(dst[:, :, 0, :], src)
                        e.tensor_copy(dst[:, :, 1, :], src)
                    to_pe(e)
                for w in range(2):
                    jobs(e, [None, shift_copy(w, 2)])
                act_copied(e)
                for w in range(2):
                    for b in range(16):
                        src = kv_shift[w][:, :, 2 * b:2 * b + CMP_STRIDE * (N_CMP - 1) + 1:CMP_STRIDE]
                        e.tensor_scalar(flat[w][:, b, :].rearrange("p (g n) -> p g n", g=NSA_G), src,
                                        pe_col[:, w, b:b + 1], None, ALU.add)
                    to_act(e)
                    from_act(e)
                    e.tensor_tensor(flat_l[w], flat[w], flat_h[w].bitcast(F32), ALU.subtract)
                    to_pe(e)
                pass_units(e, 8)
                for w in range(2):
                    if w:
                        pass_units(e, 8, {1: [rope_piece(0, 1024, 4, True)], 3: [rope_piece(1, 1024, 4)]})
                    c.add("chunk")
                    e.wait_ge(evac_act, c.at("chunk", 2))
                    e.sem_inc(evac_dve, 1)
                jobs(e, small_jobs(plain))
                for s in range(2):
                    def gated(kind):
                        def write(e, t, o):
                            g = nsa_gate[:, t, :].rearrange("p (h k) -> p h k", k=3)[:, s * NH:(s + 1) * NH, kind]
                            e.tensor_tensor(fac[:, 0:NH], rsum[:, t * NH:(t + 1) * NH], g, ALU.mult)
                            e.drain()
                            tmp = mod_a[:, 2560:3072].rearrange("p (h d) -> p h d", h=NH)
                            e.tensor_tensor(tmp, o, over_heads(fac[:, 0:NH], NH, HD), ALU.mult)
                            e.drain()
                            dst = work[:, t, s * 512:(s + 1) * 512].rearrange("p (h d) -> p h d", h=NH)
                            e.tensor_tensor(dst, dst, tmp, ALU.add)
                            e.drain()
                        return write
                    for kind in range(2):
                        to_pe(e)
                        softmax_heads(e, NSA_G, HD, 0.125, gated(1 + kind), s if kind == 0 else False,
                                      new_q=kind == 0)
                to_pe(e)
                turn(e, yh, yl, KB)
                for n in range(2):
                    def read(e, b):
                        w = slice(n * 512, (n + 1) * 512)
                        return e.scalar_tensor_tensor(x[:, :, w], x[:, :, w], ALPHA, ps[:, b:b + 2, :], ALU.mult, ALU.add)
                    chunk(e, D, read, [lambda e: half_moments(e, 0)] if n else ())
                layer_norm(e)

            def cmp_softmax(e, s):
                c.add("score")
                e.wait_ge(score_ready, c.at("score"))
                n = NH * N_CMP
                for t in range(NT):
                    v = cmp_p[:, t * n:(t + 1) * n].rearrange("p (h k) -> p h k", h=NH)
                    e.scalar_tensor_tensor(v, ps[:, 4, t * n:(t + 1) * n].rearrange("p (h k) -> p h k", h=NH), 0.125,
                                           row_over_heads(k_("cmp_mask")[:, t * N_CMP:(t + 1) * N_CMP], NH),
                                           ALU.mult, ALU.add)
                e.drain()
                whole = cmp_p[:, 0:2 * n].rearrange("p (h k) -> p h k", h=2 * NH)
                e.tensor_reduce(fac[:, 0:16], whole, AX, ALU.max)
                e.drain()
                e.tensor_tensor(whole, whole, over_heads(fac[:, 0:16], 16, N_CMP), ALU.subtract)
                to_act(e)
                from_act(e)
                for t in range(NT):
                    v = cmp_p[:, t * n:(t + 1) * n].rearrange("p (h k) -> p h k", h=NH)
                    e.tensor_tensor(v, v, row_over_heads(k_("cmp_valid")[:, t * N_CMP:(t + 1) * N_CMP], NH), ALU.mult)
                e.drain()
                e.tensor_reduce(fac[:, 0:16], whole, AX, ALU.add)
                e.drain()
                e.tensor_scalar(fac[:, 0:16], fac[:, 0:16], 1e-30, None, ALU.max)
                e.drain()
                e.reciprocal(fac[:, 0:16], fac[:, 0:16])
                e.drain()
                for t in range(NT):
                    g = nsa_gate[:, t, :].rearrange("p (h k) -> p h k", k=3)[:, s * NH:(s + 1) * NH, 0]
                    e.tensor_tensor(fac[:, t * NH:(t + 1) * NH], fac[:, t * NH:(t + 1) * NH], g, ALU.mult)
                e.drain()
                e.tensor_tensor(whole, whole, over_heads(fac[:, 0:16], 16, N_CMP), ALU.mult)
                to_pe(e)

            def cmp_output(e, s):
                jobs(e, [plain(cmp_pT[:, t, h:h + 4, :],
                               lambda bank: ps[0:N_CMP, bank, :].rearrange("p (h s) -> p h s", h=4))
                         for t in range(NT) for h in (0, 4)])
                c.add("pv")
                e.wait_ge(pv_ready, c.at("pv"))
                e.tensor_copy(work[:, :, s * 512:(s + 1) * 512], ps[:, 4:6, :])
                to_pe(e)

            def experts(e):
                turn(e, xh, xl, KB, by_tile=True)
                e.wait_ge(extra_small, 80)
                to_act(e)
                from_act(e)
                e.tensor_tensor(router_l, router, router_h.bitcast(F32), ALU.subtract)
                e.drain()
                to_act(e)
                from_act(e)
                e.tensor_tensor(xtl, x[:, :, :], xth.bitcast(F32), ALU.subtract)
                to_pe(e)
                jobs(e, [plain(logitT, lambda bank: ps[0:N_EXP, bank, 0:S])]
                     + [plain(logit[:, t, :], lambda bank: ps[:, bank, 0:N_EXP]) for t in range(NT)])
                act_copied(e)
                for t in range(NT):
                    other = logit[:, t, :].rearrange("p (o f) -> p o f", o=1).broadcast_to([P, N_EXP, N_EXP])
                    own = logit[:, t, :].rearrange("p (e o) -> p e o", o=1).broadcast_to([P, N_EXP, N_EXP])
                    e.tensor_tensor(cmp_a[:, t], other, own, ALU.is_gt)
                    e.tensor_tensor(cmp_b[:, t], other, own, ALU.is_equal)
                e.drain()
                for t in range(NT):
                    e.tensor_tensor(cmp_b[:, t], cmp_b[:, t], k_("lower_index").rearrange("p (e f) -> p e f", e=N_EXP), ALU.mult)
                e.drain()
                for t in range(NT):
                    e.tensor_tensor(cmp_a[:, t], cmp_a[:, t], cmp_b[:, t], ALU.add)
                e.drain()
                for t in range(NT):
                    e.tensor_reduce(sel[:, t, :], cmp_a[:, t], AX, ALU.add)
                e.tensor_reduce(rt[:, 32:34], logit, AX, ALU.max)
                e.drain()
                e.tensor_scalar(sel, sel, 2.0, None, ALU.is_lt)
                for t in range(NT):
                    e.tensor_scalar(rt[:, t * 8:(t + 1) * 8], logit[:, t, :], rt[:, 32 + t:33 + t], None, ALU.subtract)
                e.drain().then_inc(src_ready, 1)
                to_act(e)
                from_act(e)
                ex = rt[:, 0:16].rearrange("p (t e) -> p t e", t=NT)
                e.tensor_tensor(gate, ex, sel, ALU.mult)
                e.drain()
                e.tensor_reduce(rt[:, 34:36], gate, AX, ALU.add)
                e.drain()
                e.reciprocal(rt[:, 36:38], rt[:, 34:36])
                e.drain()
                for t in range(NT):
                    e.tensor_scalar(gate[:, t, :], gate[:, t, :], rt[:, 36 + t:37 + t], None, ALU.mult)
                jobs(e, [plain(place[:, t, :], lambda bank: ps[:, bank, 0:16]) for t in range(NT)])
                act_copied(e)
                e.tensor_reduce(rt[:, 38:39], place[:, 0, N_EXP:2 * N_EXP], AX, ALU.max)
                e.drain()
                e.tensor_scalar(rt[:, 39:40], rt[:, 38:39], float(CAP), 1.0, ALU.is_gt, ALU.add)
                e.drain()
                e.tensor_copy(rounds[0:1, 0:1], rt[0:1, 39:40])
                e.tensor_scalar(x[:, :, :], x[:, :, :], ALPHA, None, ALU.mult)
                e.drain()
                to_pe(e)
                to_act(e)
                e.sem_inc(rounds_ready, 1)
                n_rounds = 1 if e is SILENT else e.value_load(rounds[0:1, 0:1], min_val=1, max_val=2)

                def tokens_of(e, i, b):
                    at = bass.ds(i, 1)
                    e.tensor_copy(now[b][:, 0:2].rearrange("p (t o) -> p t o", o=1), place[:, :, at])
                    e.tensor_copy(now[b][:, 2:4].rearrange("p (t o) -> p t o", o=1), sel[:, :, at])
                    e.tensor_copy(now[b][:, 4:6].rearrange("p (t o) -> p t o", o=1), gate[:, :, at])
                    e.drain()
                    for t in range(NT):
                        e.tensor_scalar(onehot[b][:, t, :], k_("iota"), now[b][:, t:t + 1], now[b][:, 2 + t:3 + t],
                                        ALU.is_equal, ALU.mult)
                    to_pe(e)

                def output(e):
                    c.add("out")
                    e.wait_ge(out_hi, c.at("out"))
                    e.tensor_tensor(el, ps[:, 2:4, :].rearrange("p b n -> p (b n)"), eh.bitcast(F32),
                                    ALU.subtract).then_inc(out_lo, 1)

                def add_output(b):
                    def part(t, n):
                        def piece(e):
                            c.add("comb")
                            e.wait_ge(comb_ready, c.at("comb"))
                            w = slice(n * 512, (n + 1) * 512)
                            e.scalar_tensor_tensor(x[:, t, w], ps[:, 4 + n, :], now[b][:, 4 + t:5 + t], x[:, t, w],
                                                   ALU.mult, ALU.add).then_inc(comb_free, 1)
                        return piece
                    return [part(t, n) for t in range(NT) for n in range(2)]

                def one_expert(e, i, b, last=False):
                    output(e)
                    pieces = {5 + n: [piece] for n, piece in enumerate(add_output(1 - b))}
                    pieces[8].append(lambda e: e.drain())
                    if not last:
                        pieces[9] = [lambda e: tokens_of(e, i + 1, 1 - b)]
                    step(e, hidden_e, EXPERT, pieces)
                    step(e, hidden_e, EXPERT, {} if last else gather_pieces(jobs, gather_jobs(plain, 1 - b)))
                    loop(e, c, D_FFE // 512 - 3, lambda e, s: step(e, hidden_e, EXPERT))
                    if not last:
                        step(e, hidden_e, EXPERT)
                    else:
                        turn(e, hidden_e[0], hidden_e[1], 4, 1)
                        pass_units(e, 4)

                def one_round(e, r):
                    tokens_of(e, 0, 0)
                    e.tensor_scalar(now[1], now[0], 0.0, None, ALU.mult)
                    e.tensor_scalar(onehotT[1][:, :], x[:, 0, 0:S], 0.0, None, ALU.mult)
                    jobs(e, gather_jobs(plain, 0))
                    pass_units(e, 8)
                    c.add("chunk")
                    make_hidden(e, EXPERT)

                    def two(e, i):
                        one_expert(e, i * 2, 0)
                        one_expert(e, i * 2 + 1, 1)
                    loop(e, c, N_EXP // 2 - 1, two)
                    one_expert(e, N_EXP - 2, 0)
                    one_expert(e, N_EXP - 1, 1, last=True)
                    output(e)
                    for piece in add_output(1):
                        piece(e)
                    e.drain()
                    e.tensor_scalar(place[:, :, 0:N_EXP], place[:, :, 0:N_EXP], -float(CAP), None, ALU.add)
                    e.drain()
                loop(e, c, n_rounds, one_round)

            dve.wait_ge(const_ready, 16)
            from_act(dve)
            col = st[:, 16:24].rearrange("p (k o) -> p k o", o=1).broadcast_to([P, KB, P])
            dve.tensor_copy(chi[:, :, :], col)
            dve.drain()
            dve.tensor_tensor(clo[:, :, :], col, chi[:, :, :].bitcast(F32), ALU.subtract)
            dve.drain().then_inc(c_ready, 1)
            dve.wait_ge(positions_ready, 16)
            angle = st[:, 32:128].rearrange("p (w t n) -> p w t n", w=2, t=NT)
            turns = att[:, 0:96].rearrange("p (w t n) -> p w t n", w=2, t=NT)
            posf = st[:, 24:26]
            dve.tensor_copy(posf, posi[:, :])
            dve.drain()
            inv = const[:, CONST_AT["inv_mla"][0]:CONST_AT["inv_mb"][1]]
            for t in range(NT):
                dve.tensor_scalar(angle[:, 0, t, :], inv, posf[:, t:t + 1], None, ALU.mult)
            dve.drain()
            big = float(1.5 * 2 ** 23)
            p1, p2 = 6.28125, 0.0019350051879882812
            p3 = float(TWO_PI - p1 - p2)
            flat_angle = [angle[:, w].rearrange("p t n -> p (t n)") for w in range(2)]
            flat_turns = [turns[:, w].rearrange("p t n -> p (t n)") for w in range(2)]
            dve.tensor_scalar(flat_turns[0], flat_angle[0], float(1.0 / TWO_PI), big, ALU.mult, ALU.add)
            dve.drain()
            dve.tensor_scalar(flat_turns[0], flat_turns[0], -big, None, ALU.add)
            dve.drain()
            for part in (p1, p2, p3):
                dve.scalar_tensor_tensor(flat_angle[0], flat_turns[0], -part, flat_angle[0], ALU.mult, ALU.add)
                dve.drain()
            dve.tensor_scalar(flat_angle[1], flat_angle[0], float(np.pi / 2), None, ALU.add)
            dve.drain()
            dve.tensor_scalar(flat_turns[1], flat_angle[1], float(np.pi), -TWO_PI, ALU.is_gt, ALU.mult)
            dve.drain()
            dve.tensor_tensor(flat_angle[1], flat_angle[1], flat_turns[1], ALU.add)
            dve.drain()
            dve.tensor_scalar(st[:, 32:128], st[:, 32:128], float(np.float32(3.1415925)), float(np.float32(-3.1415925)),
                              ALU.min, ALU.max)
            to_act(dve)
            from_act(dve)
            for w, (a_mla, a_mb) in enumerate(((16, 40), (0, 32))):
                dve.tensor_copy(rope_tab[:, :, a_mla:a_mla + 16], angle[:, w, :, 0:16])
                dve.tensor_copy(rope_tab[:, :, a_mb:a_mb + 8], angle[:, w, :, 16:24])
            dve.drain()
            for u in range(LEAD):
                split(dve, u)

            def two(e, i):
                e.wait_ge(bias_ready[0], 16)
                for side in range(2):
                    at = bass.ds((0 if isinstance(i, int) else i * D) + side * 512, 512)
                    chunk(e, D, lambda e, b: e.tensor_tensor(mod_a[:, at], ps[:, b, :], mod_a[:, at], ALU.add))
            loop(dve, c, 2, two)
            dve.wait_ge(x_ready, 16)
            dve.sem_inc(dve_tick, 1)
            for _ in range(NT):
                to_act(dve)
            c.add("bias0")
            loop(dve, c, DEPTH, layer)
            rms_final(dve)
            retention(dve)
            turn(dve, xh, xl, KB, by_tile=True)
            mlp(dve, (yh, yl), D_FF2, SWIGLU)
            add_mlp(dve)
            layer_norm(dve)
            sparse_attention(dve)
            experts(dve)
            half_moments(dve, 0)
            layer_norm(dve, final=True)
            dve.sem_inc(x_done, 1)

        extra_used, rounds_ready = sem("extra_used"), sem("rounds_ready")
        last_gain, x_done = sem("last_gain"), sem("x_done")

        def sp_program(sp, c):
            def load(e, src):
                slot, _ = c.slot()
                e.wait_ge(split_lo, c.at("unit", 1))
                dst = raw[:, slot, :].rearrange("p (j n) -> p j n", j=src.shape[1])
                e.dma_start(dst[:, :, 0:src.shape[2]], src).then_inc(raw_ready[slot], 16)
                c.add("unit")

            def rows(w, at, blocks=UROWS):
                return w[bass.ds(at, blocks * P), :].rearrange("(j p) n -> p j n", p=P)

            def columns(e, w, n_rows, first, width=UCOLS):
                for i in range(units_of(n_rows)):
                    load(e, rows(w, i * UROWS * P)[:, :, bass.ds(first, width)])

            def mlp_in(e, w_in, width, kind, s, units=range(8)):
                wide = kind[0]
                for u in units:
                    if kind is SWIGLU and u < 4:
                        load(e, rows(w_in, u % 2 * 512, 4)[:, :, bass.ds(s * wide + u // 2 * width, wide)])
                    elif kind is EXPERT or u < 4:
                        load(e, rows(w_in, u % 4 * 256)[:, :, bass.ds(s * wide + u // 4 * width, wide)])

            def mlp_out(e, w_out, kind, s):
                for kg in range(kind[0] // 256):
                    for n in range(2):
                        load(e, rows(w_out, s * kind[0] + kg * 256)[:, :, n * 512:(n + 1) * 512])

            def mlp(e, w_in, w_out, width, kind):
                steps, pair = width // kind[0], kind[2]
                mlp_in(e, w_in, width, kind, 0)

                def body(e, i):
                    for k in range(pair):
                        mlp_in(e, w_in, width, kind, i * pair + (k + 1))
                        mlp_out(e, w_out, kind, i * pair + k)
                loop(e, c, (steps - 1) // pair, body)
                for s in range((steps - 1) // pair * pair, steps - 1):
                    mlp_in(e, w_in, width, kind, s + 1)
                    mlp_out(e, w_out, kind, s)
                mlp_out(e, w_out, kind, steps - 1)

            def layer(e, l):
                w_in = a["w_in"][l]
                for half in range(2):
                    if half:
                        mlp(e, a["w_ff1"][l], a["w_ff2"][l], D_FF, RELU2)
                        break
                    columns(e, w_in, D, 0)
                    columns(e, w_in, D, 512)
                    columns(e, w_in, D, 1024, ROPE)
                    for branch, w_o in enumerate(("w_o_mla", "w_o_sb", "w_o_moba")):
                        if branch:
                            for i in range(3):
                                columns(e, w_in, D, (IN_SB, IN_MB)[branch - 1] + i * 512)
                        for n in range(2):
                            columns(e, w_in, D, IN_GATES + branch * D + n * 512)
                        if branch == 0:
                            columns(e, a["w_uq"][l], Q_RANK, 0)
                            columns(e, a["w_uq"][l], Q_RANK, 512, 256)
                            columns(e, a["w_ukv"][l], KV_RANK, 0)
                            columns(e, a["w_ukv"][l], KV_RANK, 512)
                        for _, _, ahead, at in fill_of[branch]:
                            columns(e, a["w_ada"][(l + ahead) % DEPTH], D, at)
                        for n in range(2):
                            columns(e, a[w_o][l], 512, n * 512)
                    for n in range(2):
                        columns(e, a["w_out"][l], D, n * 512)

            def experts(e):
                w_in, w_out = a["moe_w_in_2"][0], a["moe_w_out_2"][0]
                mlp_in(e, w_in[0], D_FFE, EXPERT, 0, range(LEAD))
                e.wait_ge(rounds_ready, 1)
                n_rounds = e.value_load(rounds[0:1, 0:1], min_val=1, max_val=2)

                def one_expert(e, i):
                    def body(e, s):
                        mlp_in(e, w_in[i], D_FFE, EXPERT, s + 1)
                        mlp_out(e, w_out[i], EXPERT, s)
                    loop(e, c, D_FFE // 512 - 1, body)
                    mlp_in(e, w_in[i + 1], D_FFE, EXPERT, 0)
                    mlp_out(e, w_out[i], EXPERT, D_FFE // 512 - 1)

                def one_round(e, r):
                    mlp_in(e, w_in[0], D_FFE, EXPERT, 0, range(LEAD, 8))
                    loop(e, c, N_EXP - 1, one_expert)

                    def body(e, s):
                        mlp_in(e, w_in[N_EXP - 1], D_FFE, EXPERT, s + 1)
                        mlp_out(e, w_out[N_EXP - 1], EXPERT, s)
                    loop(e, c, D_FFE // 512 - 1, body)
                    mlp_out(e, w_out[N_EXP - 1], EXPERT, D_FFE // 512 - 1)
                    mlp_in(e, w_in[0], D_FFE, EXPERT, 0, range(LEAD))
                loop(e, c, n_rounds, one_round)

            sp.dma_start(const[:, :], consts).then_inc(const_ready, 16)
            sp.dma_start(st[:, 16:24], a["c"].rearrange("o (k p) -> p (o k)", p=P),
                         allow_slow_non_contiguous=True).then_inc(c_ready, 16)
            sp.dma_start(posi[:, :], a["positions"].rearrange("o (t p) -> p (o t)", p=P),
                         allow_slow_non_contiguous=True).then_inc(positions_ready, 16)
            loop(sp, c, 2, lambda e, i: [columns(e, a["w_ada"][0], D, i * D + side * 512) for side in range(2)])
            sp.dma_start(x[:, :, :], a["x"].rearrange("o (t p) n -> p (o t) n", p=P)).then_inc(x_ready, 16)
            loop(sp, c, DEPTH, layer)
            for part in range(3):
                loop(sp, c, 2, lambda e, i: [columns(e, a["ret_w_in_2"][0], D, i * D + (part * 2048 + side * 512))
                                             for side in range(2)])
            for kg in range(8):
                for n in range(2):
                    load(sp, rows(a["ret_w_out_2"][0], kg * 256)[:, :, n * 512:(n + 1) * 512])
            mlp(sp, a["ffn_w_in_2"][0], a["ffn_w_out_2"][0], D_FF2, SWIGLU)
            for i in range(2):
                columns(sp, a["nsa_w_q_2"][0], D, i * 512)
            columns(sp, a["nsa_w_q_2"][0], D, 1024, 48)
            for i in range(3):
                columns(sp, a["nsa_w_kv_2"], D, i * 512)
            columns(sp, a["cmp_k_w1_2"], 2048, 0, CMP_HID)
            columns(sp, a["cmp_v_w1_2"], 2048, 0, CMP_HID)
            for n in range(2):
                columns(sp, a["nsa_w_out_2"][0], D, n * 512)
            experts(sp)
            sp.wait_ge(x_done, 1)
            sp.dma_start(out.rearrange("o (t p) n -> p (o t) n", p=P), x[:, :, :]).then_inc(stored, 16)
            sp.wait_ge(stored, 16)

        def pool_program(pool, c):
            def broadcast(v, n):
                return v.rearrange("(o n) -> o n", o=1).broadcast_to([P, n])

            def after(e, used, name):
                c.add(name)
                e.wait_ge(used, c.at(name))
                e.sem_inc(pool_tick, 1)

            pool.memset(zero[:, :], 0.0).then_inc(zero_ready, 1)
            for s, n in ((split_lo, RING), (unit_used, RING), (evac_act, 2), (evac_dve, 2), (t_lo, 2), (job_act, 1),
                         (job_dve, 1), (comb_free, 2), (gain_a_used, 1), (gain_b_used, 1), (bias_used[0], 1), (bias_used[1], 1), (bias_used[2], 1)):
                pool.sem_inc(s, n)

            def load_bias(e, l, region):
                buf, to, at = ((mod_a[:, 0:2 * D], 2 * D, 0), (mod_a[:, 2 * D:3 * D], 3 * D, 2 * D),
                               (mod_b[:, :], 6 * D, 3 * D))[region]
                after(e, bias_used[region], f"bias{region}")
                e.dma_start(buf, broadcast(a["b_ada"][l][at:to], to - at)).then_inc(bias_ready[region], 16)

            def layer(e, l):
                after(e, gain_a_used, "ga")
                e.dma_start(gain_a[:, :], broadcast(a["norm1_g"][l], D)).then_inc(gain_a_ready, 16)
                load_bias(e, l, 1)
                after(e, gain_b_used, "gb")
                e.dma_start(gain_b[:, 0:768], broadcast(a["q_norm_g"][l], 768)).then_inc(gain_b_ready, 16)
                e.dma_start(gain_b[:, 768:1024], broadcast(a["kv_norm_g"][l], 256)).then_inc(gain_b_ready, 16)
                load_bias(e, l, 2)
                after(e, gain_a_used, "ga")
                e.dma_start(gain_a[:, :], broadcast(a["norm2_g"][l], D)).then_inc(gain_a_ready, 16)
                load_bias(e, (l + 1) % DEPTH, 0)

            load_bias(pool, 0, 0)
            loop(pool, c, DEPTH, layer)
            after(pool, gain_a_used, "ga")
            pool.dma_start(gain_a[:, :], broadcast(a["final_norm_g"], D)).then_inc(gain_a_ready, 16)
            for i in range(4):
                after(pool, gain_a_used, "ga")
                if i == 0:
                    pool.dma_start(mod_a[:, 0:1024], decays).then_inc(extra_ready, 16)
                    pool.dma_start(mod_a[:, 1024:3072], broadcast(a["ret_gn_g_2"][0], 2048)).then_inc(extra_ready, 16)
                ready = gain_a_ready if i < 3 else last_gain
                pool.dma_start(gain_a[:, :], broadcast(a["ln_g_2"][i // 2][i % 2], D)).then_inc(ready, 16)
                after(pool, gain_b_used, "gb")
                ready = gain_b_ready if i < 3 else last_gain
                pool.dma_start(gain_b[:, :], broadcast(a["ln_b_2"][i // 2][i % 2], D)).then_inc(ready, 16)
                if i == 0:
                    pool.wait_ge(extra_used, 1)
                    pool.dma_start(cmp_w2[:, 0], a["cmp_k_w2_2"].rearrange("(b p) n -> p b n", p=P)).then_inc(extra_small, 16)
                    pool.dma_start(cmp_w2[:, 1], a["cmp_v_w2_2"].rearrange("(b p) n -> p b n", p=P)).then_inc(extra_small, 16)
                    for w, pe in enumerate(("cmp_k_pe_2", "cmp_v_pe_2")):
                        pool.dma_start(pe_col[:, w, :], a[pe].rearrange("(b r) d -> (r d) b", r=2),
                                       allow_slow_non_contiguous=True).then_inc(extra_small, 16)
                    pool.dma_start(router, a["moe_router_2"][0].rearrange("(k p) n -> p k n", p=P)).then_inc(extra_small, 16)

        extra_small = sem("extra_small")

        block = ctx.enter_context(nc.Block())

        @block.gpsimd
        def _(pool):
            pool_program(pool, Counts())

        @block.sync
        def _(sp):
            sp_program(sp, Counts())

        @block.tensor
        def _(pe):
            pe_program(pe, Counts())

        @block.scalar
        def _(act):
            act_program(act, Counts())

        @block.vector
        def _(dve):
            dve_program(dve, Counts())


NAMES = ["x", "c", "positions", "w_ada", "b_ada", "norm1_g", "norm2_g", "w_in", "q_norm_g", "w_uq", "kv_norm_g",
         "w_ukv", "w_o_mla", "w_o_sb", "w_o_moba", "w_out", "w_ff1", "w_ff2", "final_norm_g", "ret_w_in_2",
         "ret_gn_g_2", "ret_w_out_2", "nsa_w_kv_2", "cmp_k_pe_2", "cmp_k_w1_2", "cmp_k_w2_2", "cmp_v_pe_2",
         "cmp_v_w1_2", "cmp_v_w2_2", "nsa_w_q_2", "nsa_w_out_2", "ffn_w_in_2", "ffn_w_out_2", "moe_router_2",
         "moe_w_in_2", "moe_w_out_2", "ln_g_2", "ln_b_2"]


def kernel(**inputs):
    import concourse.bacc as bacc
    from concourse.bass_utils import run_bass_kernel_spmd

    nc = bacc.Bacc("TRN2", target_bir_lowering=False, num_devices=1)
    const, decay = shape_constants()
    arrays = {f"in_{n}": np.ascontiguousarray(inputs[n]) for n in NAMES}
    arrays["in_const"], arrays["in_decay"] = const, decay
    aps = {n: nc.dram_tensor(n, v.shape, mybir.dt.from_np(v.dtype), kind="ExternalInput").ap()
           for n, v in arrays.items()}
    out = nc.dram_tensor("out_0", (1, S, D), F32, kind="ExternalOutput").ap()
    program(nc, {n: aps[f"in_{n}"] for n in NAMES}, aps["in_const"], aps["in_decay"], out)
    r = run_bass_kernel_spmd(nc, [arrays], core_ids=[0])
    return r.results[0]["out_0"]
```
